# Optimizing a Trainium2 kernel written in Bass

```python
import math
import jax, jax.numpy as jnp
from jax import lax
import numpy as np

D_MODEL = 1024
BATCH = 1
SEQ = 2048
DEPTH = 1

CHUNK = 64
Q_BLOCK = 128
D_MIX = D_MODEL
D_ATTN = D_MIX // 2
D_RWKV = D_MIX - D_ATTN
DH_A = 64
DV_A = 2 * DH_A
H_A = D_ATTN // DV_A
ROT_DIM = DH_A // 4
ROPE_THETA = 500000.0
QK_NORM_EPS = 1e-6
SUBLN_EPS = 1e-5
RWKV_HEAD = 64
H_R = D_RWKV // RWKV_HEAD
DECAY_LORA = 64
AAA_LORA = 64
GATE_LORA = 128
LN_X_EPS = 64e-5
RWKV_COLS = 3 * D_RWKV + DECAY_LORA + AAA_LORA + GATE_LORA
D_IN = 3 * D_ATTN + RWKV_COLS
N_GROUPS = 4
EXPERTS_PER_GROUP = 8
N_EXPERTS = N_GROUPS * EXPERTS_PER_GROUP
TOP_K = 2
D_EXPERT = 512
MOE_BLOCK = 128
NORM_EPS = 1e-6

kernel_name = 'hymba_diffattn_rwkv7_hmoe_block'

def rms_norm(x, g, eps):
    xf = x.astype(jnp.float32)
    y = xf * lax.rsqrt(jnp.mean(xf * xf, axis=-1, keepdims=True) + eps)
    return (y * g.astype(jnp.float32)).astype(x.dtype)

def rope_tables(seq):
    inv = ROPE_THETA ** (-jnp.arange(0, ROT_DIM, 2, dtype=jnp.float32) / ROT_DIM)
    ang = jnp.arange(seq, dtype=jnp.float32)[:, None] * inv[None, :]
    return jnp.cos(ang), jnp.sin(ang)

def partial_rope(t, cos, sin):
    half = ROT_DIM // 2
    c = cos[None, :, None, None, :].astype(t.dtype)
    s = sin[None, :, None, None, :].astype(t.dtype)
    x1 = t[..., :half]
    x2 = t[..., half:ROT_DIM]
    return jnp.concatenate([x1 * c - x2 * s, x2 * c + x1 * s, t[..., ROT_DIM:]], axis=-1)

def diff_attention(q, k, v, lam):
    b, s = q.shape[0], q.shape[1]
    nb = s // Q_BLOCK
    scale = DH_A ** -0.5
    qb = q.reshape(b, nb, Q_BLOCK, H_A, 2, DH_A).transpose(1, 0, 2, 3, 4, 5)
    key_chunk = jnp.arange(s) // CHUNK

    def one_block(args):
        q_blk, i = args
        sc = jnp.einsum('bqhcd,bkhcd->bhcqk', q_blk, k).astype(jnp.float32) * scale
        q_chunk = (i * Q_BLOCK + jnp.arange(Q_BLOCK)) // CHUNK
        allowed = key_chunk[None, :] <= q_chunk[:, None]
        sc = jnp.where(allowed, sc, jnp.finfo(jnp.float32).min)
        p = jax.nn.softmax(sc, axis=-1)
        p_diff = p[:, :, 0] - lam * p[:, :, 1]
        return jnp.einsum('bhqk,bkhe->bqhe', p_diff.astype(v.dtype), v)

    o = lax.map(one_block, (qb, jnp.arange(nb)))
    return o.transpose(1, 0, 2, 3, 4).reshape(b, s, H_A, DV_A)

def diff_attn_mixer(u, cos, sin, q_norm_g, k_norm_g, lq1, lk1, lq2, lk2, subln_g, lambda_init):
    f32 = jnp.float32
    b, s, _ = u.shape
    q = u[..., :D_ATTN].reshape(b, s, H_A, 2, DH_A)
    k = u[..., D_ATTN:2 * D_ATTN].reshape(b, s, H_A, 2, DH_A)
    v = u[..., 2 * D_ATTN:].reshape(b, s, H_A, DV_A)
    q = partial_rope(rms_norm(q, q_norm_g, QK_NORM_EPS), cos, sin)
    k = partial_rope(rms_norm(k, k_norm_g, QK_NORM_EPS), cos, sin)
    lam = (jnp.exp(jnp.sum(lq1.astype(f32) * lk1.astype(f32)))
           - jnp.exp(jnp.sum(lq2.astype(f32) * lk2.astype(f32))) + lambda_init)
    o = diff_attention(q, k, v, lam)
    o = rms_norm(o, subln_g, SUBLN_EPS) * (1.0 - lambda_init)
    return o.reshape(b, s, D_ATTN)

def rwkv7_mixer(u, shift_mu, w0, w_lora_up, a0, a_lora_up, g_lora_up, k_k, k_a, r_k, ln_x_g, ln_x_b):
    f32 = jnp.float32
    b, s, _ = u.shape
    u_prev = jnp.concatenate([jnp.zeros_like(u[:, :1]), u[:, :-1]], axis=1)
    u = u + (u_prev - u) * shift_mu
    r = u[..., :D_RWKV]
    k = u[..., D_RWKV:2 * D_RWKV]
    v = u[..., 2 * D_RWKV:3 * D_RWKV]
    o = 3 * D_RWKV
    w_lo = u[..., o:o + DECAY_LORA]
    a_lo = u[..., o + DECAY_LORA:o + DECAY_LORA + AAA_LORA]
    g_lo = u[..., o + DECAY_LORA + AAA_LORA:]
    w = -jax.nn.softplus(-(w0.astype(f32) + (jnp.tanh(w_lo) @ w_lora_up).astype(f32))) - 0.5
    decay = jnp.exp(-jnp.exp(w))
    a = jax.nn.sigmoid(a0.astype(f32) + (a_lo @ a_lora_up).astype(f32))
    g = jax.nn.sigmoid(g_lo) @ g_lora_up
    kk = (k.astype(f32) * k_k.astype(f32)).reshape(b, s, H_R, RWKV_HEAD)
    kk = kk / jnp.maximum(jnp.linalg.norm(kk, axis=-1, keepdims=True), 1e-12)
    k_mod = k.astype(f32) * (1.0 + (a - 1.0) * k_a.astype(f32))
    heads = lambda t: t.astype(f32).reshape(b, s, H_R, RWKV_HEAD)
    r_h, k_h, v_h, w_h, a_h = heads(r), heads(k_mod), heads(v), heads(decay), heads(a)
    b_h = kk * a_h

    def step(state, inp):
        r_t, w_t, k_t, v_t, kk_t, b_t = inp
        sa = jnp.einsum('bhvk,bhk->bhv', state, -kk_t)
        state = (state * w_t[:, :, None, :] + sa[..., None] * b_t[:, :, None, :]
                 + v_t[..., None] * k_t[:, :, None, :])
        return state, jnp.einsum('bhvk,bhk->bhv', state, r_t)

    tm = lambda t: jnp.moveaxis(t, 1, 0)
    state0 = jnp.zeros((b, H_R, RWKV_HEAD, RWKV_HEAD), f32)
    _, y = lax.scan(step, state0, (tm(r_h), tm(w_h), tm(k_h), tm(v_h), tm(kk), tm(b_h)))
    y = jnp.moveaxis(y, 0, 1)
    mu = jnp.mean(y, axis=-1, keepdims=True)
    var = jnp.mean(jnp.square(y - mu), axis=-1, keepdims=True)
    y = ((y - mu) * lax.rsqrt(var + LN_X_EPS)).reshape(b, s, D_RWKV)
    y = y * ln_x_g.astype(f32) + ln_x_b.astype(f32)
    bonus = jnp.sum(r_h * k_h * r_k.astype(f32).reshape(H_R, RWKV_HEAD), axis=-1, keepdims=True) * v_h
    y = (y + bonus.reshape(b, s, D_RWKV)) * g.astype(f32)
    return y.astype(u.dtype)

def hier_moe(h, w_rg, b_rg, w_re, b_re, w_gate, w_up, w_down):
    f32 = jnp.float32
    b, s, d = h.shape
    n = b * s
    t = h.reshape(n, d)
    gprob = jax.nn.softmax((t @ w_rg).astype(f32) + b_rg.astype(f32), axis=-1)
    p_group, gsel = lax.top_k(gprob, 1)
    elog = ((t @ w_re).astype(f32) + b_re.astype(f32)).reshape(n, N_GROUPS, EXPERTS_PER_GROUP)
    elog_sel = elog[jnp.arange(n), gsel[:, 0]]
    top_p, top_i = lax.top_k(jax.nn.softmax(elog_sel, axis=-1), TOP_K)
    gate = p_group * top_p / jnp.sum(top_p, axis=-1, keepdims=True)
    eid = gsel * EXPERTS_PER_GROUP + top_i

    flat_e = eid.reshape(-1)
    order = jnp.argsort(flat_e)
    sorted_e = flat_e[order]
    tok = order // TOP_K
    counts = jnp.bincount(flat_e, length=N_EXPERTS)
    padded = (counts + MOE_BLOCK - 1) // MOE_BLOCK * MOE_BLOCK
    pad_ends = jnp.cumsum(padded)
    pad_starts = pad_ends - padded
    starts = jnp.cumsum(counts) - counts
    dest = pad_starts[sorted_e] + (jnp.arange(n * TOP_K) - starts[sorted_e])
    m_pad = n * TOP_K + N_EXPERTS * MOE_BLOCK
    n_blocks = m_pad // MOE_BLOCK
    xs = jnp.zeros((m_pad, d), t.dtype).at[dest].set(t[tok])
    block_e = jnp.minimum(jnp.searchsorted(pad_ends, jnp.arange(n_blocks) * MOE_BLOCK, side='right'),
                          N_EXPERTS - 1)

    def expert_block(args):
        xb, e = args
        return (jax.nn.silu(xb @ w_gate[e]) * (xb @ w_up[e])) @ w_down[e]

    y_pad = lax.map(expert_block, (xs.reshape(n_blocks, MOE_BLOCK, d), block_e)).reshape(m_pad, d)
    dest_by_slot = jnp.zeros((n * TOP_K,), dest.dtype).at[order].set(dest)
    y_slots = y_pad[dest_by_slot].reshape(n, TOP_K, d)
    y = jnp.einsum('nkd,nk->nd', y_slots, gate.astype(y_slots.dtype))
    return y.reshape(b, s, d)

def setup_inputs(seed: int = 0) -> dict:
    key = jax.random.key(seed)
    ks = iter(jax.random.split(key, 32))
    f32 = jnp.float32
    L = DEPTH
    nrm = lambda shape, sc: jax.random.normal(next(ks), shape, f32) * sc
    uni = lambda shape, lo, hi: jax.random.uniform(next(ks), shape, f32, lo, hi)
    return {
        'x': nrm((BATCH, SEQ, D_MODEL), 1.0),
        'ln1_g': 1.0 + nrm((L, D_MODEL), 0.02),
        'w_in': nrm((L, D_MODEL, D_IN), D_MODEL ** -0.5),
        'q_norm_g': 1.0 + nrm((L, DH_A), 0.02),
        'k_norm_g': 1.0 + nrm((L, DH_A), 0.02),
        'lambda_q1': nrm((L, DH_A), 0.1),
        'lambda_k1': nrm((L, DH_A), 0.1),
        'lambda_q2': nrm((L, DH_A), 0.1),
        'lambda_k2': nrm((L, DH_A), 0.1),
        'subln_g': 1.0 + nrm((L, DV_A), 0.02),
        'shift_mu': uni((L, RWKV_COLS), 0.0, 1.0),
        'w0': uni((L, D_RWKV), -6.5, -1.5),
        'w_lora_up': nrm((L, DECAY_LORA, D_RWKV), 0.1),
        'a0': nrm((L, D_RWKV), 0.1),
        'a_lora_up': nrm((L, AAA_LORA, D_RWKV), AAA_LORA ** -0.5),
        'g_lora_up': nrm((L, GATE_LORA, D_RWKV), GATE_LORA ** -0.5),
        'k_k': 0.85 + nrm((L, D_RWKV), 0.02),
        'k_a': 1.0 + nrm((L, D_RWKV), 0.02),
        'r_k': nrm((L, D_RWKV), 0.1),
        'ln_x_g': 1.0 + nrm((L, D_RWKV), 0.02),
        'ln_x_b': nrm((L, D_RWKV), 0.02),
        'w_out': nrm((L, D_MIX, D_MODEL), D_MIX ** -0.5),
        'ln2_g': 1.0 + nrm((L, D_MODEL), 0.02),
        'w_router_group': nrm((L, D_MODEL, N_GROUPS), D_MODEL ** -0.5),
        'b_router_group': nrm((L, N_GROUPS), 0.01),
        'w_router_expert': nrm((L, D_MODEL, N_EXPERTS), D_MODEL ** -0.5),
        'b_router_expert': nrm((L, N_EXPERTS), 0.01),
        'w_exp_gate': nrm((L, N_EXPERTS, D_MODEL, D_EXPERT), D_MODEL ** -0.5),
        'w_exp_up': nrm((L, N_EXPERTS, D_MODEL, D_EXPERT), D_MODEL ** -0.5),
        'w_exp_down': nrm((L, N_EXPERTS, D_EXPERT, D_MODEL), D_EXPERT ** -0.5),
    }

def reference(x, ln1_g, w_in, q_norm_g, k_norm_g, lambda_q1, lambda_k1, lambda_q2, lambda_k2, subln_g,
              shift_mu, w0, w_lora_up, a0, a_lora_up, g_lora_up, k_k, k_a, r_k, ln_x_g, ln_x_b,
              w_out, ln2_g, w_router_group, b_router_group, w_router_expert, b_router_expert,
              w_exp_gate, w_exp_up, w_exp_down):
    cos, sin = rope_tables(x.shape[1])
    h = x
    for l in range(DEPTH):
        lambda_init = 0.8 - 0.6 * math.exp(-0.3 * l)
        u = rms_norm(h, ln1_g[l], NORM_EPS) @ w_in[l]
        o_a = diff_attn_mixer(u[..., :3 * D_ATTN], cos, sin, q_norm_g[l], k_norm_g[l],
                              lambda_q1[l], lambda_k1[l], lambda_q2[l], lambda_k2[l],
                              subln_g[l], lambda_init)
        o_b = rwkv7_mixer(u[..., 3 * D_ATTN:], shift_mu[l], w0[l], w_lora_up[l], a0[l],
                          a_lora_up[l], g_lora_up[l], k_k[l], k_a[l], r_k[l], ln_x_g[l], ln_x_b[l])
        h = h + jnp.concatenate([o_a, o_b], axis=-1) @ w_out[l]
        h = h + hier_moe(rms_norm(h, ln2_g[l], NORM_EPS), w_router_group[l], b_router_group[l],
                         w_router_expert[l], b_router_expert[l], w_exp_gate[l], w_exp_up[l],
                         w_exp_down[l])
    return h


_drawn_inputs = setup_inputs


def setup_inputs(seed=0):
    import zlib

    import numpy as np

    out = dict(_drawn_inputs(seed))
    spreads = {}
    factors = {'k_norm_g': 8.992,
     'lambda_q1': 64.0,
     'w_lora_up': 2.739,
     'a0': 2.672,
     'k_k': 10.58,
     'k_a': 3.524,
     'ln_x_g': 9.498,
     'ln_x_b': 3.942,
     'b_router_group': 18.569,
     'b_router_expert': 13.527,
     'q_norm_g': 2.687,
     'lambda_k2': 3.045,
     'subln_g': 4.393,
     'ln2_g': 3.472}
    for name, (base, spread) in spreads.items():
        noise = np.random.default_rng([zlib.crc32(name.encode()), seed]).standard_normal(out[name].shape)
        drawn = base * np.exp(spread * noise) if base else spread * noise
        out[name] = __import__('jax').numpy.asarray(drawn.astype(out[name].dtype))
    for name, factor in factors.items():
        out[name] = (out[name] * factor).astype(out[name].dtype)
    return out
```

```python
from contextlib import ExitStack

import concourse.bass as bass
from concourse import mybir
import numpy as np

F32 = mybir.dt.float32
I32 = mybir.dt.int32
U32 = mybir.dt.uint32
ACT = mybir.ActivationFunctionType
ALU = mybir.AluOpType
AX = mybir.AxisListType.X

P = 128
D = 1024
S = 2048
KC = D // P
GT = 256
NG = S // GT
NT = S // P
DA = 512
H_A = 4
RW = 1792
RT = RW // P
NPAIR = 4
C = 64
NCH = S // C
CPG = GT // C
ROW = 5 * C + 1
N_IN = 3 * DA + RW
NE = 32
EPG = 8
DE = 512
NB = 2 * S // P + NE
E_HALF = float(np.exp(-0.5))
LAMBDA_INIT = 0.8 - 0.6 * float(np.exp(-0.3 * 0))

PC_LN1, PC_MU, PC_W0, PC_A0, PC_KK, PC_KA, PC_RK, PC_LXG, PC_LXB, PC_LN2, PC_QG, PC_KG = (
    0, 8, 22, 26, 30, 34, 38, 42, 46, 50, 58, 59)
PC_N = 60


class Pool:

    def __init__(self, nc, ctx, tag):
        self.nc, self.ctx, self.tag = nc, ctx, tag

    def sb(self, name, shape, dt=F32):
        return self.ctx.enter_context(self.nc.sbuf_tensor(f"{self.tag}_{name}", shape, dt))

    def ps(self, name, shape, dt=F32):
        return self.ctx.enter_context(self.nc.psum_tensor(f"{self.tag}_{name}", shape, dt))

    def sem(self, name):
        return self.ctx.enter_context(self.nc.semaphore(f"{self.tag}_{name}"))


class Count:

    def __init__(self, sem, turn, per):
        self.sem, self.turn, self.per, self.n = sem, turn, per, 0

    def at(self, n):
        return self.turn * self.per + n

    def step(self, ins):
        self.n += 1
        ins.then_inc(self.sem, 1)

    def end(self, what):
        assert self.n == self.per, (what, self.n, self.per)


def link(eng, count, ins):
    count.step(ins)
    eng.wait_ge(count.sem, count.at(count.n))


def wide(ap, n):
    return ap.unsqueeze(2).broadcast_to([ap.shape[0], ap.shape[1], n])


def middle(ap, n):
    return ap.unsqueeze(1).broadcast_to([ap.shape[0], n, ap.shape[1]])


MAIN = [("mix", 12), ("mix", 13)]
for _p in range(NPAIR):
    MAIN += [("mix", 4 + _p), ("mix", _p), ("mix", 8 + _p)]
MAIN += [("qk", _i) for _i in range(8)] + [("v", _t) for _t in range(GT // P)]
NM = len(MAIN)
AUX_A = {j: [] for j in range(NM)}
AUX_D = {j: [] for j in range(NM)}
for _p in range(NPAIR):
    AUX_A[4 + 3 * _p] += [("w", _p), ("a", _p), ("g", _p)]
    AUX_A[6 + 3 * _p] += [("kk", _p)]
    AUX_D[7 + 3 * _p] += [("bonus", _p)]
for _i in range(8):
    AUX_A[15 + _i] += [("norm", _i)]
    AUX_D[16 + _i] += [("turn", _i)]
ORDER_A = [x for j in range(NM) for x in AUX_A[j]]
ORDER_D = [x for j in range(NM) for x in AUX_D[j]]
NA, ND = len(ORDER_A), len(ORDER_D)
XT = GT // P


def project(nc, io, dr):
    with ExitStack() as ctx:
        m = Pool(nc, ctx, "pj")
        w_in = m.sb("w_in", [P, KC, N_IN])
        xnT = m.sb("xnT", [P, KC, GT])
        xt = m.sb("xt", [P, XT, D])
        junk = m.sb("junk", [P, D])
        ident = m.sb("ident", [P, P])
        ones2 = m.sb("ones2", [P, P])
        swap = m.sb("swap", [P, P])
        cols = m.sb("cols", [P, PC_N])
        ncol = m.sb("ncol", [P, 14])
        loras = m.sb("loras", [P, 2, DA])
        cosin = m.sb("cosin", [P, 2, GT])
        reset = m.sb("reset", [P, GT])
        stat = m.sb("stat", [P, 3, XT])
        eps = m.sb("eps", [P, 1])
        carry = m.sb("carry", [P, RT])
        ubuf = m.sb("ubuf", [P, 2, GT])
        lo = m.sb("lo", [P, 2, GT])
        lot = m.sb("lot", [P, 2, GT])
        krv = m.sb("krv", [P, 2, 3, GT])
        za = m.sb("za", [P, 2, GT])
        cz = m.sb("cz", [P, GT])
        dec = m.sb("dec", [P, 3, GT])
        gout = m.sb("gout", [P, GT])
        kk = m.sb("kk", [P, 2, GT])
        ksq = m.sb("ksq", [P, GT])
        kn = m.sb("kn", [P, GT])
        kmod = m.sb("kmod", [P, GT])
        rk = m.sb("rk", [P, GT])
        bon = m.sb("bon", [P, GT])
        st = m.sb("st", [P, CPG, ROW])
        qr = m.sb("qr", [P, 2, GT])
        qsq = m.sb("qsq", [P, 2, GT])
        qrr = m.sb("qrr", [P, 2, GT])
        qn = m.sb("qn", [P, 2, GT])
        m1 = m.sb("m1", [P, GT])
        m2 = m.sb("m2", [P, GT])
        qo = m.sb("qo", [P, GT])
        vo = m.sb("vo", [P, DA])

        tp = m.ps("tp", [P, KC, P])
        big = [m.ps(f"big{i}", [P, 512]) for i in range(2)]
        aux_a = [m.ps(f"aux_a{i}", [P, 512]) for i in range(2)]
        aux_d = [m.ps(f"aux_d{i}", [P, 512]) for i in range(2)]

        s_const = m.sem("const")
        s_ncol = m.sem("ncol")
        s_x = [m.sem(f"x{i}") for i in range(XT)]
        s_cs = m.sem("cs")
        s_rms = m.sem("rms")
        s_rstd = m.sem("rstd")
        s_xs = m.sem("xs")
        s_tp = m.sem("tp_done")
        s_xnT = m.sem("xnT_done")
        s_main = m.sem("main")
        s_evac = m.sem("evac")
        s_mixed = m.sem("mixed")
        s_tanh = m.sem("tanh")
        s_eg = m.sem("eg")
        s_sig = m.sem("sig")
        s_kk0 = m.sem("kk0")
        s_ksq = m.sem("ksq_done")
        s_scan = m.sem("scan")
        s_dec = m.sem("dec_done")
        s_rk = m.sem("rk_done")
        s_prep = m.sem("prep")
        s_qn = m.sem("qn_done")
        s_qo = m.sem("qo_done")
        s_aa = m.sem("aa")
        s_aa_free = m.sem("aa_free")
        s_ad = m.sem("ad")
        s_ad_free = m.sem("ad_free")
        s_act = m.sem("act")
        s_dve = m.sem("dve")
        o_st, o_bon, o_g, o_q, o_v = (m.sem(n) for n in ("o_st", "o_bon", "o_g", "o_q", "o_v"))
        block = ctx.enter_context(nc.Block())

        w_v = io["w_in"][0].rearrange("(k p) n -> p k n", p=P)
        consts = [(ident[:, :], io["c_ident"]), (ones2[:, :], io["c_ones2"]), (swap[:, :], io["c_swap"]),
                  (cols[:, :], io["cols"]), (reset[:, :], io["c_reset"]),
                  (loras[0:64, 0, :], io["w_lora_up"][0]), (loras[64:128, 0, :], io["a_lora_up"][0]),
                  (loras[:, 1, :], io["g_lora_up"][0]),
                  (w_in[:, :, 3 * DA:], w_v[:, :, 3 * DA:]), (w_in[:, :, 0:3 * DA], w_v[:, :, 0:3 * DA])]
        N_CONST = 16 * len(consts)

        @block.sync
        def _(sp):
            for t in range(XT):
                sp.dma_start(xt[:, t, :], io["x"][t * P:(t + 1) * P, :]).then_inc(s_x[t], 16)
            for dst, src in consts:
                sp.dma_start(dst, src).then_inc(s_const, 16)
            with sp.Fori(0, NG) as g:
                sp.wait_ge(s_qo, 8 * g + 1)
                sp.dma_start(cosin[:, :, :], io["c_cosin"][:, :, bass.ds(g * GT, GT)]).then_inc(s_cs, 16)
                for t in range(XT):
                    sp.wait_ge(s_tp, XT * g + t + 1)
                    sp.dma_start(xt[:, t, :], io["x"][bass.ds(g * GT + GT + t * P, P), :]).then_inc(s_x[t], 16)
                for j, (kind, i) in enumerate(MAIN):
                    for what, p in AUX_A[j]:
                        if what == "g":
                            sp.wait_ge(s_aa_free, NA * g + ORDER_A.index((what, p)) + 3)
                            sp.dma_start(dr["g"][p, :, bass.ds(g * GT, GT)], gout[:, :]).then_inc(o_g, 16)
                        if what == "kk":
                            sp.wait_ge(s_prep, 4 * g + p + 2)
                            sp.dma_start(dr["chunks"][bass.ds(g * CPG, CPG), :, p, :].rearrange("c p n -> p c n"),
                                         st[:, :, :]).then_inc(o_st, 16)
                    for what, p in AUX_D[j]:
                        if what == "bonus":
                            sp.wait_ge(s_ad_free, ND * g + ORDER_D.index((what, p)) + 3)
                            sp.dma_start(dr["bonus"][p, :, bass.ds(g * GT, GT)], bon[:, :]).then_inc(o_bon, 16)
                        if what == "turn":
                            sp.wait_ge(s_qo, 8 * g + p + 2)
                            sp.dma_start(dr["qk"][p, :, bass.ds(g * GT, GT)], qo[:, :]).then_inc(o_q, 16)
                    if kind == "v":
                        sp.wait_ge(s_evac, NM * g + j + 3)
                        sp.dma_start(dr["v"][bass.ds(g * GT + i * P, P), :], vo[:, :]).then_inc(o_v, 16)
            for sem, n in ((o_g, 4), (o_st, 4), (o_bon, 4), (o_q, 8), (o_v, XT)):
                sp.wait_ge(sem, 16 * n * NG + 16)
            for t in range(XT):
                sp.wait_ge(s_x[t], 16 * NG + 16)

        @block.tensor
        def _(pe):
            pe.wait_ge(s_const, N_CONST)
            pe.wait_ge(s_ncol, 1)
            pe.sem_inc(s_main, 1)
            with pe.Fori(0, NG) as g:
                for t in range(XT):
                    pe.wait_ge(s_xs, XT * g + t + 1)
                    pe.wait_ge(s_xnT, XT * g + t + 1)
                    for k in range(KC):
                        ins = pe.transpose(tp[:, k, :], xt[:, t, k * P:(k + 1) * P], ident[:, :])
                    ins.then_inc(s_tp, 1)
                pe.wait_ge(s_xnT, XT * g + XT + 1)
                na = nd = 0
                for j, (kind, i) in enumerate(MAIN):
                    pe.wait_ge(s_evac, NM * g + j + 1)
                    for k in range(KC):
                        if kind == "v":
                            out, lhs, rhs = big[j % 2][:, 0:DA], xnT[:, k, i * P:(i + 1) * P], w_in[:, k, 2 * DA:3 * DA]
                        else:
                            c0 = 3 * DA + i * P if kind == "mix" else i * P
                            out, lhs, rhs = big[j % 2][:, 0:GT], w_in[:, k, c0:c0 + P], xnT[:, k, :]
                        ins = pe.matmul(out, lhs, rhs, start=(k == 0), stop=(k == KC - 1))
                    ins.then_inc(s_main, 1)
                    for what, p in AUX_A[j]:
                        pe.wait_ge(s_aa_free, NA * g + na + 1)
                        out = aux_a[na % 2][:, 0:GT]
                        cs = slice(p * P, (p + 1) * P)
                        if what == "w":
                            pe.wait_ge(s_tanh, g + 1)
                            lhs, rhs = loras[0:64, 0, cs], lot[0:64, 0, :]
                        elif what == "a":
                            pe.wait_ge(s_mixed, RT * g + 3)
                            lhs, rhs = loras[64:128, 0, cs], lo[64:128, 0, :]
                        elif what == "g":
                            pe.wait_ge(s_sig, g + 1)
                            lhs, rhs = loras[:, 1, cs], lot[:, 1, :]
                        elif what == "kk":
                            pe.wait_ge(s_ksq, 4 * g + p + 1)
                            lhs, rhs = ones2[:, :], ksq[:, :]
                        else:
                            pe.wait_ge(s_evac, NM * g + 14 + p + 3)
                            lhs, rhs = ones2[:, :], qsq[:, p % 2, :]
                        pe.matmul(out, lhs, rhs, start=True, stop=True).then_inc(s_aa, 1)
                        na += 1
                    for what, p in AUX_D[j]:
                        pe.wait_ge(s_ad_free, ND * g + nd + 1)
                        if what == "bonus":
                            pe.wait_ge(s_rk, 4 * g + p + 1)
                            lhs, rhs = ones2[:, :], rk[:, :]
                        else:
                            pe.wait_ge(s_qn, 8 * g + p + 3)
                            lhs, rhs = swap[:, :], qn[:, p % 2, :]
                        pe.matmul(aux_d[nd % 2][:, 0:GT], lhs, rhs, start=True, stop=True).then_inc(s_ad, 1)
                        nd += 1

        @block.scalar
        def _(act):
            act.sem_inc(s_evac, 2)
            act.sem_inc(s_aa_free, 2)
            act.sem_inc(o_g, 16)
            act.sem_inc(o_v, 16)
            act.wait_ge(s_const, N_CONST)
            act.wait_ge(s_ncol, 1)
            with act.Fori(0, NG) as g:
                ch = Count(s_act, g, XT)
                for t in range(XT):
                    act.wait_ge(s_x[t], 16 * g + 16)
                    link(act, ch, act.activation(junk[:, :], xt[:, t, :], ACT.Square, accum_out=stat[:, 0, t:t + 1]))
                    act.activation(stat[:, 1, t:t + 1], stat[:, 0, t:t + 1], ACT.Sqrt, bias=eps[:, :],
                                   scale=1.0 / D).then_inc(s_rms, 1)
                    act.wait_ge(s_rstd, XT * g + t + 1)
                    act.activation(xt[:, t, :], xt[:, t, :], ACT.Copy, scale=stat[:, 2, t:t + 1]).then_inc(s_xs, 1)
                na = 0
                for j, (kind, i) in enumerate(MAIN):
                    act.wait_ge(s_main, NM * g + j + 2)
                    if kind == "mix":
                        act.wait_ge(s_mixed, RT * g + j + 1)
                        act.activation(ubuf[:, j % 2, :], big[j % 2][:, 0:GT], ACT.Copy).then_inc(s_evac, 1)
                    elif kind == "qk":
                        act.wait_ge(s_qn, 8 * g + i + 1)
                        act.activation(qr[:, i % 2, :], big[j % 2][:, 0:GT], ACT.Copy)
                        act.activation(qsq[:, i % 2, :], big[j % 2][:, 0:GT], ACT.Square).then_inc(s_evac, 1)
                    else:
                        act.wait_ge(o_v, 16 * XT * g + 16 * i + 16)
                        act.activation(vo[:, :], big[j % 2][:, 0:DA], ACT.Copy).then_inc(s_evac, 1)
                    if j == 0:
                        act.wait_ge(s_mixed, RT * g + 3)
                        act.activation(lot[0:64, 0, :], lo[0:64, 0, :], ACT.Tanh).then_inc(s_tanh, 1)
                    if j == 1:
                        act.wait_ge(s_mixed, RT * g + 4)
                        act.activation(lot[:, 1, :], lo[:, 1, :], ACT.Exp, scale=-1.0).then_inc(s_eg, 1)
                    if j < 14 and j % 3 == 1 and j >= 4:
                        act.wait_ge(s_kk0, 4 * g + (j - 4) // 3 + 1)
                        act.activation(ksq[:, :], kk[:, (j - 4) // 3 % 2, :], ACT.Square).then_inc(s_ksq, 1)
                    if 5 <= j <= 14 and j % 3 == 2:
                        p = (j - 5) // 3
                        act.wait_ge(s_scan, 4 * g + p + 1)
                        act.activation(dec[:, 0, :], cz[:, :], ACT.Exp, scale=-E_HALF)
                        act.activation(dec[:, 1, :], za[:, 0, :], ACT.Exp, scale=-E_HALF)
                        act.activation(dec[:, 2, :], cz[:, :], ACT.Exp, scale=E_HALF).then_inc(s_dec, 1)
                    for what, p in AUX_A[j]:
                        act.wait_ge(s_aa, NA * g + na + 1)
                        src = aux_a[na % 2][:, 0:GT]
                        if what == "w":
                            act.wait_ge(s_prep, 4 * g + p + 1)
                            ins = act.activation(za[:, 0, :], src, ACT.Exp, bias=ncol[:, p:p + 1], scale=-1.0)
                        elif what == "a":
                            ins = act.activation(za[:, 1, :], src, ACT.Exp, bias=ncol[:, 4 + p:5 + p], scale=-1.0)
                        elif what == "g":
                            act.wait_ge(o_g, 64 * g + 16 * p + 16)
                            ins = act.activation(gout[:, :], src, ACT.Copy)
                        elif what == "kk":
                            ins = act.activation(kn[:, :], src, ACT.Sqrt)
                        else:
                            ins = act.activation(qrr[:, p % 2, :], src, ACT.Sqrt, bias=eps[:, :], scale=1.0 / 64)
                        ins.then_inc(s_aa_free, 1)
                        na += 1
                ch.end("project, ScalarE")

        @block.vector
        def _(dve):
            for sem, n in ((s_xnT, 1), (s_mixed, 2), (s_prep, 1), (s_qn, 2), (s_qo, 1), (s_ad_free, 2),
                           (o_st, 16), (o_bon, 16), (o_q, 16)):
                dve.sem_inc(sem, n)
            dve.memset(carry[:, :], 0.0)
            dve.memset(eps[:, :], 1e-6)
            dve.wait_ge(s_const, N_CONST)
            dve.tensor_scalar(ncol[:, 0:8], cols[:, PC_W0:PC_W0 + 8], -1.0, None, ALU.mult)
            dve.tensor_scalar(ncol[:, 12:13], cols[:, PC_QG:PC_QG + 1], 0.125, None, ALU.mult)
            dve.tensor_copy(ncol[:, 13:14], cols[:, PC_KG:PC_KG + 1])
            dve.tensor_scalar(ncol[:, 8:12], cols[:, PC_KA:PC_KA + 4], -1.0, 1.0, ALU.mult, ALU.add).then_inc(s_ncol, 1)
            dve.wait_ge(s_ncol, 1)
            with dve.Fori(0, NG) as g:
                ch = Count(s_dve, g, 2 * RT - 14 + 1 + 4 * 8 + 8 * 2)

                def chunked(ap):
                    return ap.rearrange("p (c n) -> p c n", n=C)

                for t in range(XT):
                    dve.wait_ge(s_rms, XT * g + t + 1)
                    dve.reciprocal(stat[:, 2, t:t + 1], stat[:, 1, t:t + 1]).then_inc(s_rstd, 1)
                dve.wait_ge(s_main, NM * g + 1)
                for t in range(XT):
                    dve.wait_ge(s_tp, XT * g + t + 1)
                    dve.tensor_tensor(xnT[:, :, t * P:(t + 1) * P], tp[:, :, :],
                                      wide(cols[:, PC_LN1:PC_LN1 + KC], P), ALU.mult).then_inc(s_xnT, 1)
                nd = 0
                for j, (kind, i) in enumerate(MAIN):
                    if kind == "mix":
                        u = ubuf[:, j % 2, :]
                        if j < 2:
                            dst = lo[:, j, :]
                        else:
                            dst = krv[:, (j - 2) // 3 % 2, (j - 2) % 3, :]
                        dve.wait_ge(s_evac, NM * g + j + 3)
                        dve.tensor_tensor(dst[:, 1:], u[:, 0:GT - 1], u[:, 1:], ALU.subtract)
                        link(dve, ch, dve.tensor_tensor(dst[:, 0:1], carry[:, i:i + 1], u[:, 0:1], ALU.subtract))
                        dve.tensor_copy(carry[:, i:i + 1], u[:, GT - 1:GT])
                        dve.scalar_tensor_tensor(dst, dst, cols[:, PC_MU + i:PC_MU + i + 1], u,
                                                 ALU.mult, ALU.add).then_inc(s_mixed, 1)
                        if j == 1:
                            dve.wait_ge(s_eg, g + 1)
                            link(dve, ch, dve.tensor_scalar(lot[:, 1, :], lot[:, 1, :], 1.0, None, ALU.add))
                            dve.reciprocal(lot[:, 1, :], lot[:, 1, :]).then_inc(s_sig, 1)
                        if j >= 2 and (j - 2) % 3 == 0:
                            p = (j - 2) // 3
                            dve.wait_ge(s_mixed, RT * g + j + 3)
                            dve.tensor_scalar(kk[:, p % 2, :], dst, cols[:, PC_KK + p:PC_KK + p + 1], None,
                                              ALU.mult).then_inc(s_kk0, 1)
                    for what, p in AUX_A[j]:
                        ready = NA * g + ORDER_A.index((what, p)) + 3
                        if what == "kk":
                            k, r, v = (krv[:, p % 2, n, :] for n in range(3))
                            dve.wait_ge(s_aa_free, ready)
                            link(dve, ch, dve.tensor_scalar(kn[:, :], kn[:, :], 1e-12, None, ALU.max))
                            link(dve, ch, dve.reciprocal(kn[:, :], kn[:, :]))
                            link(dve, ch, dve.tensor_tensor(kk[:, p % 2, :], kk[:, p % 2, :], kn[:, :], ALU.mult))
                            dve.wait_ge(s_dec, 4 * g + p + 1)
                            dve.wait_ge(o_st, 64 * g + 16 * p + 16)
                            link(dve, ch, dve.tensor_tensor(za[:, 1, :], kk[:, p % 2, :], za[:, 1, :], ALU.mult))
                            dve.scalar_tensor_tensor(st[:, :, 0:C], chunked(kk[:, p % 2, :]), -1.0,
                                                     chunked(dec[:, 1, :]), ALU.mult, ALU.mult)
                            dve.tensor_tensor(st[:, :, C:2 * C], chunked(r), chunked(dec[:, 0, :]), ALU.mult)
                            dve.tensor_tensor(st[:, :, 2 * C:3 * C], chunked(za[:, 1, :]), chunked(dec[:, 2, :]), ALU.mult)
                            dve.tensor_tensor(st[:, :, 3 * C:4 * C], chunked(kmod[:, :]), chunked(dec[:, 2, :]), ALU.mult)
                            dve.tensor_copy(st[:, :, 4 * C:5 * C], chunked(v))
                            dve.tensor_copy(st[:, :, 5 * C:5 * C + 1], chunked(dec[:, 0, :])[:, :, C - 1:C]).then_inc(s_prep, 1)
                        if what == "norm":
                            dve.wait_ge(s_aa_free, ready)
                            link(dve, ch, dve.reciprocal(qrr[:, p % 2, :], qrr[:, p % 2, :]))
                            gain = ncol[:, 12 + p // 4:13 + p // 4]
                            dve.scalar_tensor_tensor(qn[:, p % 2, :], qr[:, p % 2, :], gain, qrr[:, p % 2, :],
                                                     ALU.mult, ALU.mult).then_inc(s_qn, 1)
                    for what, p in AUX_D[j]:
                        dve.wait_ge(s_ad, ND * g + nd + 1)
                        src = aux_d[nd % 2][:, 0:GT]
                        nd += 1
                        if what == "bonus":
                            dve.wait_ge(o_bon, 64 * g + 16 * p + 16)
                            dve.tensor_tensor(bon[:, :], src, krv[:, p % 2, 2, :], ALU.mult).then_inc(s_ad_free, 1)
                        else:
                            if p == 0:
                                dve.wait_ge(s_cs, 16 * g + 16)
                            dve.wait_ge(s_qo, 8 * g + p + 1)
                            dve.tensor_tensor(m2[:, :], src, cosin[:, 1, :], ALU.mult).then_inc(s_ad_free, 1)
                            link(dve, ch, dve.tensor_tensor(m1[:, :], qn[:, p % 2, :], cosin[:, 0, :], ALU.mult))
                            dve.wait_ge(o_q, 128 * g + 16 * p + 16)
                            dve.tensor_tensor(qo[:, :], m1[:, :], m2[:, :], ALU.add).then_inc(s_qo, 1)
                    for what, p in AUX_A[j]:
                        if what == "w":
                            k, r = krv[:, p % 2, 0, :], krv[:, p % 2, 1, :]
                            dve.wait_ge(s_aa_free, NA * g + ORDER_A.index(("a", p)) + 3)
                            link(dve, ch, dve.tensor_scalar(za[:, :, :], za[:, :, :], 1.0, None, ALU.add))
                            link(dve, ch, dve.reciprocal(za[:, :, :], za[:, :, :]))
                            dve.tensor_scalar(kmod[:, :], za[:, 1, :], cols[:, PC_KA + p:PC_KA + p + 1],
                                              ncol[:, 8 + p:9 + p], ALU.mult, ALU.add)
                            link(dve, ch, dve.tensor_tensor_scan(cz[:, :], reset[:, :], za[:, 0, :], 0.0, ALU.mult, ALU.add))
                            dve.tensor_tensor(za[:, 0, :], cz[:, :], za[:, 0, :], ALU.subtract).then_inc(s_scan, 1)
                            link(dve, ch, dve.tensor_tensor(kmod[:, :], k, kmod[:, :], ALU.mult))
                            dve.scalar_tensor_tensor(rk[:, :], r, cols[:, PC_RK + p:PC_RK + p + 1], kmod[:, :],
                                                     ALU.mult, ALU.mult).then_inc(s_rk, 1)
                ch.end("project, VectorE")


UNITS = [(i, s) for i in range(NT) for s in range(i // 4 + 1)]
NU = len(UNITS)
SEG = 4 * P


def width(i, s):
    return min(SEG, (i + 1) * P - s * SEG)


LAG = 6
RE = 8


def attention_steps():
    steps = []
    for k in range(NU + LAG + 1):
        if k < NU:
            steps += [("scores", *UNITS[k])]
        if 0 <= k + 1 - LAG < NU:
            steps += [("combine", *UNITS[k + 1 - LAG])]
        if k < NU:
            steps += [("soft", *UNITS[k])]
        if 1 <= k <= NU and (k == NU or UNITS[k][1] == 0):
            steps += [("stats", UNITS[k - 1][0], 0)]
        if 0 <= k - LAG < NU:
            steps += [("turn", *UNITS[k - LAG])]
        if 0 <= k - LAG - 1 < NU:
            i, s = UNITS[k - LAG - 1]
            steps += [("values", i, s)] + ([("out", i, 0)] if s == i // 4 else [])
    return steps


def attend(nc, io, dr):
    with ExitStack() as ctx:
        m = Pool(nc, ctx, "at")
        qz = m.sb("qz", [P, 2, S])
        kT = m.sb("kT", [P, S])
        vh = m.sb("vh", [P, NT, P])
        ident = m.sb("ident", [P, P])
        mask = m.sb("mask", [P, 2, P])
        lams = m.sb("lams", [P, 4, 64])
        lam = m.sb("lam", [P, 8])
        sign = m.sb("sign", [P, 2])
        e = m.sb("e", [P, RE, 2, SEG])
        pd = m.sb("pd", [P, 4, SEG])
        tt = m.sb("tt", [P, 2, SEG])
        pt = m.sb("pt", [P, 2, SEG])
        osb = m.sb("osb", [P, 2, P])
        nmx = m.sb("nmx", [P, RE, 2, 4])
        sums = m.sb("sums", [P, RE, 2, 4])
        f = m.sb("f", [P, RE, 2, 4])
        cf = m.sb("cf", [P, RE, 2, 4])
        small = m.sb("small", [P, 4, 2])

        zero = m.sb("zero", [P, D])

        sc = [m.ps(f"sc{n}", [P, 2, SEG]) for n in range(2)]
        ptp = [m.ps(f"ptp{n}", [P, SEG]) for n in range(2)]
        op = [m.ps(f"op{n}", [P, 512]) for n in range(2)]

        s_const = m.sem("const")
        s_zero, o_zero = m.sem("zero_done"), m.sem("o_zero")
        s_sign = m.sem("sign_done")
        s_lam = m.sem("lam_chain")
        s_ld = m.sem("ld")
        s_qz = m.sem("qz_zero")
        s_ldv = m.sem("ldv")
        s_sc = m.sem("scores")
        s_mx = m.sem("mx")
        s_exp = m.sem("exp")
        s_df = m.sem("df")
        s_f = m.sem("f_done")
        s_cf = m.sem("cf_done")
        s_t = m.sem("t")
        s_pd = m.sem("pd_done")
        s_tr = m.sem("tr")
        s_pt = m.sem("pt_done")
        s_pv = m.sem("pv")
        s_o = m.sem("o")
        s_dve = m.sem("dve")
        o_o = [m.sem(f"o_o{n}") for n in range(2)]
        block = ctx.enter_context(nc.Block())
        STEPS = attention_steps()

        @block.gpsimd
        def _(pool):
            pool.memset(zero[:, :], 0.0).then_inc(s_zero, 1)
            pool.wait_ge(s_zero, 1)
            pool.dma_start(dr["slots"][NE * P:, :].rearrange("(n p) d -> p n d", p=P),
                           zero[:, :].unsqueeze(1).broadcast_to([P, NB - NE, D])).then_inc(o_zero, 16)
            pool.wait_ge(o_zero, 16)

        def unit(i, s):
            return UNITS.index((i, s))

        def units_before(i):
            return UNITS.index((i, 0)) if i >= 0 else UNITS.index((i + NT, 0)) - NU

        @block.sync
        def _(sp):
            for dst, src in ((ident[:, :], io["c_ident"]), (mask[:, :, :], io["c_mask"]), (lams[:, :, :], io["lams"])):
                sp.dma_start(dst, src).then_inc(s_const, 16)
            sp.wait_ge(s_qz, 1)
            with sp.Fori(0, H_A) as h:
                sp.wait_ge(s_sc, NU * h + 1)
                for c in range(2):
                    rows = slice(64 * c, 64 * c + 64)
                    sp.dma_start(qz[rows, c, :], dr["qk"][bass.ds(h, 1), rows, :].rearrange("a p n -> (a p) n"))\
                        .then_inc(s_ld, 16)
                sp.dma_start(kT[:, :], dr["qk"][bass.ds(h + H_A, 1)].rearrange("a p n -> (a p) n")).then_inc(s_ld, 16)
                sp.wait_ge(s_pv, NU * h + NU)
                sp.dma_start(vh[:, :, :], dr["v"][:, bass.ds(h * P, P)].rearrange("(t p) n -> p t n", p=P))\
                    .then_inc(s_ldv, 16)
                for i in range(NT):
                    sp.wait_ge(s_o, NT * h + i + NT + 1)
                    sp.dma_start(dr["o"][i * P:(i + 1) * P, bass.ds(h * P, P)], osb[:, i % 2, :])\
                        .then_inc(o_o[i % 2], 16)
            for n in range(2):
                sp.wait_ge(o_o[n], 16 * NT // 2 * H_A + 16)

        @block.tensor
        def _(pe):
            pe.sem_inc(s_sc, 1)
            pe.sem_inc(s_tr, NU)
            pe.sem_inc(s_pv, NU)
            pe.wait_ge(s_const, 48)
            pe.wait_ge(s_sign, 1)
            with pe.Fori(0, H_A) as h:
                pe.wait_ge(s_ld, 48 * h + 48)
                for kind, i, s in STEPS:
                    if kind == "scores":
                        u, w = unit(i, s), width(i, s)
                        pe.wait_ge(s_exp, NU * h + u + 1)
                        for c in range(2):
                            diag = s == i // 4
                            ins = pe.matmul(sc[u % 2][:, c, 0:w], qz[:, c, i * P:(i + 1) * P],
                                            kT[:, s * SEG:s * SEG + w], start=True, stop=not diag)
                            if diag:
                                ins = pe.matmul(sc[u % 2][:, c, w - P:w], mask[:, 0, :], mask[:, 1, :],
                                                start=False, stop=True)
                        ins.then_inc(s_sc, 1)
                    if kind == "turn":
                        u = unit(i, s)
                        pe.wait_ge(s_pd, NU * h + NU + u + 1)
                        pe.wait_ge(s_pt, NU * h + NU + u - 1)
                        for b in range(width(i, s) // P):
                            ins = pe.transpose(ptp[u % 2][:, b * P:(b + 1) * P],
                                               pd[:, u % 4, b * P:(b + 1) * P], ident[:, :])
                        ins.then_inc(s_tr, 1)
                    if kind == "values":
                        u = unit(i, s)
                        pe.wait_ge(s_pt, NU * h + NU + u + 1)
                        if u == 0:
                            pe.wait_ge(s_ldv, 16 * h + 16)
                        if s == 0:
                            pe.wait_ge(s_o, NT * h + NT + i - 1)
                        for b in range(width(i, s) // P):
                            n = 4 * s + b
                            ins = pe.matmul(op[i % 2][:, 0:P], pt[:, u % 2, b * P:(b + 1) * P], vh[:, n, :],
                                            start=(n == 0), stop=(n == i))
                        ins.then_inc(s_pv, 1)

        @block.scalar
        def _(act):
            act.sem_inc(s_exp, 2)
            act.sem_inc(s_pt, NU)
            act.wait_ge(s_lam, 3)
            act.activation(lam[:, 2:4], lam[:, 0:2], ACT.Exp).then_inc(s_lam, 1)
            with act.Fori(0, H_A) as h:
                for kind, i, s in STEPS:
                    if kind == "soft":
                        u, w = unit(i, s), width(i, s)
                        act.wait_ge(s_mx, NU * h + u + 1)
                        act.wait_ge(s_pd, NU * h + NU + u + 1 - RE)
                        for c in range(2):
                            ins = act.activation(e[:, u % RE, c, 0:w], sc[u % 2][:, c, 0:w], ACT.Exp,
                                                 bias=nmx[:, i % RE, c, s:s + 1], accum_out=sums[:, i % RE, c, s:s + 1])
                        ins.then_inc(s_exp, 1)
                    if kind == "stats":
                        n = i // 4 + 1
                        act.wait_ge(s_df, NT * h + i + 1)
                        act.activation(f[:, i % RE, :, 0:n], f[:, i % RE, :, 0:n], ACT.Exp).then_inc(s_f, 1)
                    if kind == "combine":
                        u, w = unit(i, s), width(i, s)
                        act.wait_ge(s_cf, NT * h + i + 1)
                        act.wait_ge(s_pd, NU * h + NU + u - 1)
                        act.activation(tt[:, u % 2, 0:w], e[:, u % RE, 1, 0:w], ACT.Copy,
                                       scale=cf[:, i % RE, 1, s:s + 1]).then_inc(s_t, 1)
                    if kind == "turn":
                        u, w = unit(i, s), width(i, s)
                        act.wait_ge(s_tr, NU * h + NU + u + 1)
                        act.wait_ge(s_pv, NU * h + NU + u - 1)
                        act.activation(pt[:, u % 2, 0:w], ptp[u % 2][:, 0:w], ACT.Copy).then_inc(s_pt, 1)

        @block.vector
        def _(dve):
            dve.sem_inc(s_pd, NU)
            dve.sem_inc(s_o, NT)
            for n in range(2):
                dve.sem_inc(o_o[n], 16)
            dve.wait_ge(s_const, 48)
            pairs = lams[:, :, :].rearrange("p (a b) n -> p a b n", b=2)
            dve.tensor_tensor(pairs[:, :, 0, :], pairs[:, :, 0, :], pairs[:, :, 1, :], ALU.mult).then_inc(s_lam, 2)
            dve.wait_ge(s_lam, 2)
            dve.tensor_reduce(lam[:, 0:2], pairs[:, :, 0, :], AX, ALU.add).then_inc(s_lam, 1)
            dve.wait_ge(s_lam, 4)
            dve.tensor_tensor(lam[:, 4:5], lam[:, 3:4], lam[:, 2:3], ALU.subtract).then_inc(s_lam, 1)
            dve.memset(sign[:, 0:1], 1.0)
            dve.memset(qz[:, :, :], 0.0).then_inc(s_qz, 1)
            dve.wait_ge(s_lam, 5)
            dve.tensor_scalar(sign[:, 1:2], lam[:, 4:5], -LAMBDA_INIT, None, ALU.add).then_inc(s_sign, 1)
            dve.wait_ge(s_sign, 1)
            with dve.Fori(0, H_A) as h:
                ch = Count(s_dve, h, 5 * NT)
                for kind, i, s in STEPS:
                    if kind == "soft":
                        u, w = unit(i, s), width(i, s)
                        dve.wait_ge(s_sc, NU * h + u + 2)
                        dve.tensor_reduce(nmx[:, i % RE, :, s], sc[u % 2][:, :, 0:w], AX, ALU.max, negate=True)\
                            .then_inc(s_mx, 1)
                    if kind == "stats":
                        n, r = i // 4 + 1, i % RE
                        nm, den, rd, rs = (small[:, k, :] for k in range(4))
                        dve.wait_ge(s_mx, NU * h + units_before(i) + n)
                        link(dve, ch, dve.tensor_reduce(nm, nmx[:, r, :, 0:n], AX, ALU.min))
                        dve.tensor_tensor(f[:, r, :, 0:n], wide(nm, n), nmx[:, r, :, 0:n], ALU.subtract).then_inc(s_df, 1)
                        dve.wait_ge(s_f, NT * h + i + 1)
                        link(dve, ch, dve.tensor_tensor(cf[:, r, :, 0:n], f[:, r, :, 0:n], sums[:, r, :, 0:n], ALU.mult))
                        link(dve, ch, dve.tensor_reduce(den, cf[:, r, :, 0:n], AX, ALU.add))
                        link(dve, ch, dve.reciprocal(rd, den))
                        link(dve, ch, dve.tensor_tensor(rs, rd, sign[:, :], ALU.mult))
                        dve.tensor_tensor(cf[:, r, :, 0:n], f[:, r, :, 0:n], wide(rs, n), ALU.mult).then_inc(s_cf, 1)
                        dve.wait_ge(s_cf, NT * h + i + 1)
                    if kind == "combine":
                        u, w = unit(i, s), width(i, s)
                        dve.wait_ge(s_t, NU * h + u + 1)
                        dve.wait_ge(s_tr, NU * h + NU + u - 3)
                        dve.scalar_tensor_tensor(pd[:, u % 4, 0:w], e[:, u % RE, 0, 0:w],
                                                 cf[:, i % RE, 0, s:s + 1], tt[:, u % 2, 0:w], ALU.mult, ALU.add)\
                            .then_inc(s_pd, 1)
                    if kind == "out":
                        dve.wait_ge(s_pv, NU * h + NU + units_before(i) + i // 4 + 1)
                        dve.wait_ge(o_o[i % 2], 8 * NT * h + 16 * (i // 2) + 16)
                        dve.tensor_copy(osb[:, i % 2, :], op[i % 2][:, 0:P]).then_inc(s_o, 1)
                ch.end("attend, VectorE")


PE_PRE = ("gb", "gl", "gk", "tok", "r1", "r2", "r3", "r4", "r5", "r6", "r7", "r8")
PE_ORDER = ("gb", "gl", "s1", "gk", "s2", "tok", "s3") + PE_PRE[4:]
ACT_PRE = ("tok", "r1", "r2", "r3", "r5", "r7")
ACT_ORDER = ("s1", "s2", "tok", "s3") + ACT_PRE[1:]
DVE_PRE = ("gb", "gl", "gk", "r2", "r3", "r4", "r6", "r8")
DVE_ORDER = ("gb", "gl", "gk", "s3") + DVE_PRE[3:]
SERIAL = ("s1", "s2", "s3")


class Pieces:

    def __init__(self, sem, order, pre, c, has_pre=True, has_serial=True):
        self.sem = sem
        self.base = len(pre) + len(order) * c if has_serial else 0
        self.names = [n for n in order if (has_pre or n in SERIAL) and (has_serial or n not in SERIAL)]

    def before(self):
        return self.base

    def after(self, name):
        return self.base + (self.names.index(name) + 1)


def recur(nc, io, dr):
    with ExitStack() as ctx:
        m = Pool(nc, ctx, "rw")
        raw = m.sb("raw", [P, 2, NPAIR, ROW])
        cin = [m.sb(f"cin{x}", [P, NPAIR, ROW]) for x in range(2)]
        eye = m.sb("eye", [P, C])
        mgb = m.sb("mgb", [P, 2 * C])
        mgk = m.sb("mgk", [P, 2 * C])
        mgl = m.sb("mgl", [P, 3, C])
        gb = [m.sb(f"gb{x}", [P, NPAIR, 2 * C]) for x in range(2)]
        gk = [m.sb(f"gk{x}", [P, NPAIR, 2 * C]) for x in range(2)]
        gl = m.sb("gl", [P, NPAIR, 3, C])
        w = m.sb("w", [P, NPAIR, 3, C])
        lu4 = m.sb("lu4", [P, 2, NPAIR, C])
        l8 = m.sb("l8", [P, NPAIR, C])
        q = [m.sb(f"q{n}", [P, NPAIR, C]) for n in range(4)]
        ty = m.sb("ty", [P, 2, 2, NPAIR, C])
        q5 = [m.sb(f"q5{x}", [P, NPAIR, C]) for x in range(2)]
        tbk = [m.sb(f"tbk{x}", [P, NPAIR, 2, C]) for x in range(2)]
        tv = [m.sb(f"tv{x}", [P, NPAIR, C]) for x in range(2)]
        sa0 = m.sb("sa0", [P, NPAIR, C])
        sa = m.sb("sa", [P, NPAIR, C])
        ds_ = m.sb("ds", [P, NPAIR, C])
        state = m.sb("state", [P, NPAIR, C])
        y = m.sb("y", [P, NPAIR, S])
        ps = [m.ps(f"ps{n}", [P, 512]) for n in range(8)]

        s_const = m.sem("const")
        s_ld = [m.sem(f"ld{x}") for x in range(2)]
        s_cin = m.sem("cin_done")
        s_pe = m.sem("pe")
        s_act = m.sem("act")
        s_dve = m.sem("dve")
        s_init = m.sem("init")
        s_dchain = m.sem("dchain")
        s_out = m.sem("out")
        s_apart, s_apart2 = m.sem("apart"), m.sem("apart2")
        block = ctx.enter_context(nc.Block())
        TURNS = NCH // 2 - 1

        def quarter(n, k):
            return ps[n][:, 256 * k:256 * k + 256].rearrange("p (a n) -> p a n", n=C)

        def pairs(n, width=2 * C):
            return ps[n][:, :].rearrange("p (a n) -> p a n", n=width)

        @block.sync
        def _(sp):
            for dst, src in ((eye[:, :], io["c_eye"]), (mgb[:, :], io["c_mgb"]), (mgk[:, :], io["c_mgk"]),
                             (mgl[:, :, :], io["c_mgl"])):
                sp.dma_start(dst, src).then_inc(s_const, 16)
            for x in range(2):
                sp.dma_start(raw[:, x], dr["chunks"][x]).then_inc(s_ld[x], 16)
            with sp.Fori(0, TURNS) as i:
                for x in range(2):
                    sp.wait_ge(s_cin, 2 * i + x + 1)
                    sp.dma_start(raw[:, x], dr["chunks"][bass.ds(2 * i + x + 2, 1)].rearrange("c p a n -> (c p) a n"))\
                        .then_inc(s_ld[x], 16)
            sp.wait_ge(s_act, len(ACT_PRE) + len(ACT_ORDER) * (NCH - 1) + 3)
            sp.dma_start(dr["y"].rearrange("a p n -> p a n"), y[:, :, :]).then_inc(s_out, 16)
            sp.wait_ge(s_out, 16)

        @block.gpsimd
        def _(pool):
            for x in range(2):
                pool.wait_ge(s_ld[x], 16)
                pool.tensor_copy(cin[x][:, :, :], raw[:, x]).then_inc(s_cin, 1)
            with pool.Fori(0, TURNS) as i:
                for x in range(2):
                    pool.wait_ge(s_ld[x], 16 * i + 32)
                    pool.wait_ge(s_pe, Pieces(s_pe, PE_ORDER, PE_PRE, 2 * i + x).after("s3"))
                    pool.wait_ge(s_dve, Pieces(s_dve, DVE_ORDER, DVE_PRE, 2 * i + x).after("s3"))
                    pool.sem_inc(s_apart2, 1)
                    pool.tensor_copy(cin[x][:, :, :], raw[:, x]).then_inc(s_cin, 1)

        HALVES = [slice(0, C), slice(C, P)]

        @block.tensor
        def _(pe):
            def half(c, x, has_pre=True, has_serial=True):
                a = Pieces(s_act, ACT_ORDER, ACT_PRE, c, has_pre, has_serial)
                d = Pieces(s_dve, DVE_ORDER, DVE_PRE, c, has_pre, has_serial)
                nx = 1 - x if has_serial else x

                def product(out, lhs, rhs, start=True, stop=True):
                    return pe.matmul(out, lhs, rhs, start=start, stop=stop)

                def every(*products):
                    pe.sem_inc(s_apart, 1)
                    for p in range(NPAIR):
                        for rows in HALVES:
                            for f in products:
                                ins = f(p, rows)
                    ins.then_inc(s_pe, 1)

                A, R, B, K, V = (slice(n * C, (n + 1) * C) for n in range(5))
                AR = slice(0, 2 * C)
                if has_pre:
                    pe.wait_ge(s_cin, c + 2 if has_serial else 1)
                    every(lambda p, r: product(pairs(0)[r, p, :], cin[nx][r, p, B], cin[nx][r, p, AR]))
                    every(lambda p, r: product(quarter(2, 0)[r, p, :], cin[nx][r, p, A], cin[nx][r, p, B]))
                if has_serial:
                    pe.wait_ge(s_dve, d.before())
                    pe.wait_ge(s_act, a.before())
                    every(lambda p, r: product(quarter(6, 0)[r, p, :], cin[x][r, p, A], state[r, p, :], stop=False),
                          lambda p, r: product(quarter(6, 0)[r, p, :], gk[x][r, p, 0:C], tv[x][r, p, :], start=False))
                if has_pre:
                    if has_serial:
                        pe.wait_ge(s_dve, d.before())
                    every(lambda p, r: product(pairs(1)[r, p, :], cin[nx][r, p, K], cin[nx][r, p, AR]))
                if has_serial:
                    pe.wait_ge(s_act, a.after("s1"))
                    every(lambda p, r: product(quarter(6, 1)[r, p, :], q5[x][r, p, :], sa0[r, p, :]))
                if has_pre:
                    every(lambda p, r: product(pairs(3)[r, p, 0:C], cin[nx][r, p, B], eye[r, :]),
                          lambda p, r: product(pairs(3)[r, p, C:2 * C], cin[nx][r, p, K], eye[r, :]),
                          lambda p, r: product(quarter(4, 0)[r, p, :], cin[nx][r, p, V], eye[r, :]))
                if has_serial:
                    pe.wait_ge(s_act, a.after("s2"))
                    if has_pre:
                        pe.wait_ge(s_dve, d.after("gl"))
                    every(lambda p, r: product(quarter(7, 0)[r, p, :], state[r, p, :], cin[x][r, p, R], stop=False),
                          lambda p, r: product(quarter(7, 0)[r, p, :], tv[x][r, p, :], gk[x][r, p, C:2 * C], False, False),
                          lambda p, r: product(quarter(7, 0)[r, p, :], sa[r, p, :], gb[x][r, p, C:2 * C], start=False),
                          lambda p, r: product(quarter(2, 0)[r, p, :], tbk[x][r, p, 0, :], sa[r, p, :], stop=False),
                          lambda p, r: product(quarter(2, 0)[r, p, :], tbk[x][r, p, 1, :], tv[x][r, p, :], start=False))
                if has_pre:
                    U = slice(0, C)
                    pe.wait_ge(s_dve, d.after("gk"))
                    every(lambda p, r: product(pairs(5)[r, p, 0:C], gl[r, p, 0, :], gb[nx][r, p, U]),
                          lambda p, r: product(pairs(5)[r, p, C:2 * C], gb[nx][r, p, U], gl[r, p, 0, :]))
                    pe.wait_ge(s_act, a.after("r1"))
                    every(lambda p, r: product(pairs(0)[r, p, :], w[r, p, 2, :], w[r, p, 0:2, :].rearrange("p a n -> p (a n)")),
                          lambda p, r: product(quarter(1, 0)[r, p, :], w[r, p, 1, :], w[r, p, 2, :]))
                    pe.wait_ge(s_act, a.after("r2"))
                    pe.wait_ge(s_dve, d.after("r2"))
                    every(lambda p, r: product(quarter(2, 0)[r, p, :], lu4[r, 0, p, :], q[0][r, p, :]),
                          lambda p, r: product(quarter(5, 0)[r, p, :], lu4[r, 1, p, :], lu4[r, 0, p, :]))
                    pe.wait_ge(s_act, a.after("r3"))
                    pe.wait_ge(s_dve, d.after("r3"))
                    every(lambda p, r: product(quarter(3, 0)[r, p, :], l8[r, p, :], q[1][r, p, :]))
                    pe.wait_ge(s_dve, d.after("r4"))
                    every(lambda p, r: product(quarter(4, 0)[r, p, :], q[2][r, p, :], eye[r, :]),
                          lambda p, r: product(quarter(4, 1)[r, p, :], gl[r, p, 1, :], q[2][r, p, :]))
                    pe.wait_ge(s_act, a.after("r5"))
                    every(lambda p, r: product(quarter(5, 0)[r, p, :], ty[r, 0, 0, p, :], ty[r, 0, 1, p, :]))
                    pe.wait_ge(s_dve, d.after("r6"))
                    every(lambda p, r: product(quarter(0, 0)[r, p, :], q[3][r, p, :], eye[r, :]),
                          lambda p, r: product(quarter(0, 1)[r, p, :], gl[r, p, 2, :], q[3][r, p, :]))
                    pe.wait_ge(s_act, a.after("r7"))
                    every(lambda p, r: product(quarter(1, 0)[r, p, :], ty[r, 1, 0, p, :], ty[r, 1, 1, p, :]))

            pe.wait_ge(s_const, 64)
            pe.wait_ge(s_init, 1)
            half(0, 0, has_serial=False)
            with pe.Fori(0, TURNS) as i:
                for x in range(2):
                    half(2 * i + x, x)
            half(NCH - 2, 0)
            half(NCH - 1, 1, has_pre=False)

        @block.scalar
        def _(act):
            def half(c, x, has_pre=True, has_serial=True):
                t = Pieces(s_pe, PE_ORDER, PE_PRE, c, has_pre, has_serial)
                nx = 1 - x if has_serial else x

                def copy(dst, src):
                    return act.activation(dst, src, ACT.Copy)

                if has_serial:
                    act.wait_ge(s_pe, t.after("s1"))
                    copy(sa0[:, :, :], quarter(6, 0)).then_inc(s_act, 1)
                    act.wait_ge(s_pe, t.after("s2"))
                    copy(sa[:, :, :], quarter(6, 1)).then_inc(s_act, 1)
                if has_pre:
                    act.wait_ge(s_pe, t.after("tok"))
                    copy(tbk[nx][:, :, :, :].rearrange("p a b n -> p a (b n)"), pairs(3))
                    copy(tv[nx][:, :, :], quarter(4, 0)).then_inc(s_act, 1)
                if has_serial:
                    act.wait_ge(s_pe, t.after("s3"))
                    copy(y[:, :, bass.ds(c * C, C)], quarter(7, 0)).then_inc(s_act, 1)
                if has_pre:
                    act.wait_ge(s_pe, t.after("r1"))
                    copy(w[:, :, 1:3, :].rearrange("p a b n -> p a (b n)"), pairs(5)).then_inc(s_act, 1)
                    act.wait_ge(s_pe, t.after("r2"))
                    copy(lu4[:, 0], quarter(1, 0)).then_inc(s_act, 1)
                    act.wait_ge(s_pe, t.after("r3"))
                    copy(l8[:, :, :], quarter(5, 0)).then_inc(s_act, 1)
                    act.wait_ge(s_pe, t.after("r5"))
                    copy(ty[:, 0].rearrange("p a b n -> p (a b n)"), ps[4][:, :]).then_inc(s_act, 1)
                    act.wait_ge(s_pe, t.after("r7"))
                    copy(ty[:, 1].rearrange("p a b n -> p (a b n)"), ps[0][:, :]).then_inc(s_act, 1)

            half(0, 0, has_serial=False)
            with act.Fori(0, TURNS) as i:
                for x in range(2):
                    half(2 * i + x, x)
            half(NCH - 2, 0)
            half(NCH - 1, 1, has_pre=False)

        @block.vector
        def _(dve):
            def half(c, x, has_pre=True, has_serial=True):
                t = Pieces(s_pe, PE_ORDER, PE_PRE, c, has_pre, has_serial)
                d = Pieces(s_dve, DVE_ORDER, DVE_PRE, c, has_pre, has_serial)
                nx = 1 - x if has_serial else x
                if has_pre:
                    dve.wait_ge(s_pe, t.after("gb"))
                    dve.tensor_tensor(gb[nx][:, :, :], pairs(0), middle(mgb[:, :], NPAIR), ALU.mult).then_inc(s_dve, 1)
                    dve.wait_ge(s_pe, t.after("gl"))
                    dve.tensor_tensor(gl[:, :, :, :], quarter(2, 0).unsqueeze(2).broadcast_to([P, NPAIR, 3, C]),
                                      mgl[:, :, :].unsqueeze(1).broadcast_to([P, NPAIR, 3, C]), ALU.mult).then_inc(s_dve, 1)
                    dve.wait_ge(s_pe, t.after("gk"))
                    dve.tensor_tensor(gk[nx][:, :, :], pairs(1), middle(mgk[:, :], NPAIR), ALU.mult)
                    dve.wait_ge(s_dve, d.after("gb"))
                    dve.tensor_tensor(w[:, :, 0, :], gb[nx][:, :, 0:C], middle(eye[:, :], NPAIR), ALU.add).then_inc(s_dve, 1)
                if has_serial:
                    dve.wait_ge(s_pe, t.after("s3"))
                    dve.tensor_tensor(ds_[:, :, :], quarter(2, 0), state[:, :, :], ALU.add).then_inc(s_dchain, 1)
                    dve.wait_ge(s_dchain, c + 1)
                    dve.tensor_tensor(state[:, :, :], ds_[:, :, :], cin[x][:, :, 5 * C:5 * C + 1].broadcast_to([P, NPAIR, C]),
                                      ALU.mult).then_inc(s_dve, 1)
                if has_pre:
                    for name, bank, old, new in (("r2", 0, w[:, :, 0, :], q[0]), ("r3", 2, q[0][:, :, :], q[1]),
                                                 ("r4", 3, q[1][:, :, :], q[2]), ("r6", 5, q[2][:, :, :], q[3]),
                                                 ("r8", 1, q[3][:, :, :], q5[nx])):
                        src = pairs(0)[:, :, 0:C] if name == "r2" else quarter(bank, 0)
                        dve.wait_ge(s_pe, t.after(name))
                        if name == "r2":
                            dve.tensor_copy(lu4[:, 1], pairs(0)[:, :, C:2 * C])
                        dve.tensor_tensor(new[:, :, :], src, old, ALU.add).then_inc(s_dve, 1)

            dve.memset(state[:, :, :], 0.0).then_inc(s_init, 1)
            dve.wait_ge(s_const, 64)
            half(0, 0, has_serial=False)
            with dve.Fori(0, TURNS) as i:
                for x in range(2):
                    half(2 * i + x, x)
            half(NCH - 2, 0)
            half(NCH - 1, 1, has_pre=False)


NEG = -1e30


def merge(nc, io, dr, keep):
    with ExitStack() as ctx:
        m = Pool(nc, ctx, "mg")
        w_out = m.sb("w_out", [P, KC, D])
        w_rt = m.sb("w_rt", [P, KC, 4 + NE])
        b_rt = m.sb("b_rt", [P, 4 + NE])
        cols = m.sb("cols", [P, PC_N])
        subln = m.sb("subln", [P, P])
        ident = m.sb("ident", [P, P])
        mean2 = m.sb("mean2", [P, P])
        giota = m.sb("giota", [P, NE])
        eiota = m.sb("eiota", [P, NE])
        eps = m.sb("eps", [P, 3])
        yin = m.sb("yin", [P, 2, 3, NPAIR, GT])
        oin = m.sb("oin", [P, 2, XT, DA])
        xin = m.sb("xin", [P, 2, XT, D])
        sq = m.sb("sq", [P, D])
        osq = m.sb("osq", [P, DA])
        rinv = m.sb("rinv", [P, D])
        ost = m.sb("ost", [P, 2, H_A])
        mix = m.sb("mix", [P, 2 * NPAIR, GT])
        hb = m.sb("hb", [P, XT, D])
        hn = m.sb("hn", [P, XT, D])
        st = m.sb("st", [P, 3, XT])
        tT = m.sb("tT", [P, KC, P])
        lg = m.sb("lg", [P, 4 + NE])
        g8 = m.sb("g8", [P, 8])
        m8 = m.sb("m8", [P, 8])
        i8 = m.sb("i8", [P, 8], U32)
        gi = m.sb("gi", [P, 1])
        eg = m.sb("eg", [P, 4])
        pen = m.sb("pen", [P, NE])
        v8 = m.sb("v8", [P, 8])
        j8 = m.sb("j8", [P, 8], U32)
        ji = m.sb("ji", [P, 2])
        sm = m.sb("sm", [P, 8])

        pm = m.ps("pm", [P, 2, 512])
        pt = m.ps("pt", [P, 512])
        pr = m.ps("pr", [P, 512])
        po = m.ps("po", [P, 2, 512])
        ph = m.ps("ph", [P, KC, P])

        s_const = m.sem("const")
        s_in = [m.sem(f"in{x}") for x in range(2)]
        s_used = m.sem("used")
        s_pe, s_act, s_dve = m.sem("pe"), m.sem("act"), m.sem("dve")
        o_h = [m.sem(f"o_h{t}") for t in range(XT)]
        o_hn = [m.sem(f"o_hn{t}") for t in range(XT)]
        block = ctx.enter_context(nc.Block())
        consts = [(w_out[:, :, :], io["w_out"][0].rearrange("(k p) n -> p k n", p=P)), (w_rt[:, :, :], io["w_rt"]),
                  (b_rt[:, :], io["b_rt"]), (cols[:, :], io["cols"]), (subln[:, :], io["subln"]),
                  (ident[:, :], io["c_ident"]), (mean2[:, :], io["c_mean2"]), (giota[:, :], io["c_giota"]),
                  (eiota[:, :], io["c_eiota"])]
        N_CONST = 16 * len(consts)

        PE_L = ["mean", "var"] + [f"{n}{t}" for t in range(XT) for n in ("oT", "proj", "hT", "route")]
        ACT_L = ["sq", "sd"] + [f"{n}{t}" for t in range(XT) for n in ("osd", "oT", "hsd", "hn", "eg", "e2")]
        DVE_L = ["init", "d", "rinv", "mixr"] + [f"{n}{t}" for t in range(XT) for n in (
            "osq", "on", "h", "rstd", "tT", "gmax", "v8", "done")]
        CHAIN_SEM = m.sem("chain")
        s_chain_a = m.sem("chain_a")
        s_apart = m.sem("apart")
        CHAIN = 3 + 17 * XT

        def pe_at(g, name):
            return len(PE_L) * g + (PE_L.index(name) + 1)

        def act_at(g, name):
            return len(ACT_L) * g + (ACT_L.index(name) + 1)

        def dve_at(g, name):
            return len(DVE_L) * g + (DVE_L.index(name) + 1)

        @block.sync
        def _(sp):
            for dst, src in consts:
                sp.dma_start(dst, src).then_inc(s_const, 16)

            def load(g, x):
                cols_g = bass.ds(g * GT, GT)
                for n, src in enumerate((dr["y"], dr["bonus"], dr["g"])):
                    sp.dma_start(yin[:, x, n], src[:, :, cols_g].rearrange("a p n -> p a n")).then_inc(s_in[x], 16)
                sp.dma_start(oin[:, x], dr["o"][cols_g, :].rearrange("(t p) n -> p t n", p=P)).then_inc(s_in[x], 16)
                sp.dma_start(xin[:, x], io["x"][cols_g, :].rearrange("(t p) n -> p t n", p=P)).then_inc(s_in[x], 16)

            load(0, 0)
            load(1, 1)

            def store(g, x):
                for t in range(XT):
                    rows = bass.ds(g * GT + t * P, P)
                    sp.wait_ge(s_dve, dve_at(g, f"h{t}"))
                    sp.dma_start(dr["h"][rows, :], hb[:, t, :]).then_inc(o_h[t], 16)
                    sp.wait_ge(s_act, act_at(g, f"hn{t}"))
                    sp.dma_start(dr["hn"][rows, :], hn[:, t, :]).then_inc(o_hn[t], 16)

            with sp.Fori(0, NG // 2 - 1) as i:
                for x in range(2):
                    g = 2 * i + x
                    store(g, x)
                    load(g + 2, x)
            for x in range(2):
                store(NG - 2 + x, x)
            for t in range(XT):
                sp.wait_ge(o_h[t], 16 * NG + 16)
                sp.wait_ge(o_hn[t], 16 * NG + 16)

        @block.tensor
        def _(pe):
            def group(g, x):
                pe.wait_ge(s_in[x], 80 * (g_turn[0] + 1))
                for n in range(2):
                    ins = pe.matmul(pm[:, n, :], mean2[:, :], yin[:, x, 0].rearrange("p a n -> p (a n)")[:, 512 * n:512 * n + 512],
                                    start=True, stop=True)
                ins.then_inc(s_pe, 1)
                pe.wait_ge(s_act, act_at(g, "sq"))
                for n in range(2):
                    ins = pe.matmul(pm[:, n, :], mean2[:, :], sq[:, 512 * n:512 * n + 512], start=True, stop=True)
                ins.then_inc(s_pe, 1)
                for t in range(XT):
                    tok = slice(t * P, (t + 1) * P)
                    pe.wait_ge(s_dve, dve_at(g, f"on{t}"))
                    for h in range(H_A):
                        ins = pe.transpose(pt[:, h * P:(h + 1) * P], oin[:, x, t, h * P:(h + 1) * P], ident[:, :])
                    ins.then_inc(s_pe, 1)
                    pe.wait_ge(s_act, act_at(g, f"oT{t}"))
                    for n in range(2):
                        for k in range(KC):
                            ins = pe.matmul(po[:, n, :], mix[:, k, tok], w_out[:, k, 512 * n:512 * n + 512],
                                            start=(k == 0), stop=(k == KC - 1))
                    ins.then_inc(s_pe, 1)
                    pe.wait_ge(s_act, act_at(g, f"hn{t}"))
                    for k in range(KC):
                        ins = pe.transpose(ph[:, k, :], hn[:, t, k * P:(k + 1) * P], ident[:, :])
                    ins.then_inc(s_pe, 1)
                    pe.wait_ge(s_dve, dve_at(g, f"tT{t}"))
                    for k in range(KC):
                        ins = pe.matmul(pr[:, 0:4 + NE], tT[:, k, :], w_rt[:, k, :], start=(k == 0), stop=(k == KC - 1))
                    ins.then_inc(s_pe, 1)

            pe.wait_ge(s_const, N_CONST)
            g_turn = [0]
            with pe.Fori(0, NG // 2) as i:
                g_turn[0] = i
                for x in range(2):
                    group(2 * i + x, x)

        @block.scalar
        def _(act):
            act.wait_ge(s_const, N_CONST)
            act.wait_ge(s_dve, 1)
            with act.Fori(0, NG // 2) as i:
                for x in range(2):
                    g = 2 * i + x
                    yf = yin[:, x, 0].rearrange("p a n -> p (a n)")
                    pmf = pm[:, :, :].rearrange("p a n -> p (a n)")
                    act.wait_ge(s_dve, dve_at(g, "d"))
                    act.activation(sq[:, :], yf, ACT.Square).then_inc(s_act, 1)
                    act.wait_ge(s_pe, pe_at(g, "var"))
                    act.activation(rinv[:, :], pmf, ACT.Sqrt, bias=eps[:, 0:1]).then_inc(s_act, 1)
                    for t in range(XT):
                        act.wait_ge(s_dve, dve_at(g, f"osq{t}"))
                        act.activation(ost[:, 1, :], ost[:, 0, :], ACT.Sqrt, bias=eps[:, 1:2], scale=1.0 / P).then_inc(s_act, 1)
                        act.wait_ge(s_pe, pe_at(g, f"oT{t}"))
                        act.activation(mix[:, 0:H_A, t * P:(t + 1) * P], pt[:, :].rearrange("p (a n) -> p a n", n=P),
                                       ACT.Copy).then_inc(s_act, 1)
                        act.wait_ge(s_dve, dve_at(g, f"h{t}"))
                        act.activation(sq[:, :], hb[:, t, :], ACT.Square, accum_out=st[:, 0, t:t + 1]).then_inc(s_chain_a, 1)
                        act.wait_ge(s_chain_a, XT * g + t + 1)
                        act.activation(st[:, 1, t:t + 1], st[:, 0, t:t + 1], ACT.Sqrt, bias=eps[:, 2:3],
                                       scale=1.0 / D).then_inc(s_act, 1)
                        act.wait_ge(s_dve, dve_at(g, f"rstd{t}"))
                        act.wait_ge(o_hn[t], 16 * g + 16)
                        act.activation(hn[:, t, :], hb[:, t, :], ACT.Copy, scale=st[:, 2, t:t + 1]).then_inc(s_act, 1)
                        act.wait_ge(s_dve, dve_at(g, f"gmax{t}"))
                        act.activation(eg[:, :], lg[:, 0:4], ACT.Exp, bias=sm[:, 0:1], accum_out=sm[:, 1:2]).then_inc(s_act, 1)
                        act.wait_ge(s_dve, dve_at(g, f"v8{t}"))
                        act.activation(sm[:, 3:4], v8[:, 1:2], ACT.Exp, bias=sm[:, 2:3]).then_inc(s_act, 1)

        @block.vector
        def _(dve):
            for t in range(XT):
                dve.sem_inc(o_h[t], 16)
                dve.sem_inc(o_hn[t], 16)
            dve.memset(eps[:, 0:1], 64e-5)
            dve.memset(eps[:, 1:2], 1e-5)
            dve.memset(eps[:, 2:3], 1e-6)
            dve.memset(g8[:, :], NEG)
            dve.wait_ge(s_const, N_CONST)
            with dve.Fori(0, NG // 2) as i:
                for x in range(2):
                    g = 2 * i + x
                    ch = Count(CHAIN_SEM, g, CHAIN)
                    yf = yin[:, x, 0].rearrange("p a n -> p (a n)")
                    pmf = pm[:, :, :].rearrange("p a n -> p (a n)")
                    dve.memset(lg[:, 0:1], 0.0).then_inc(s_dve, 1)
                    dve.wait_ge(s_in[x], 80 * i + 80)
                    dve.wait_ge(s_pe, pe_at(g, "mean"))
                    dve.tensor_tensor(yf, yf, pmf, ALU.subtract).then_inc(s_dve, 1)
                    dve.wait_ge(s_act, act_at(g, "sd"))
                    dve.reciprocal(rinv[:, :], rinv[:, :]).then_inc(s_dve, 1)
                    dve.wait_ge(s_dve, dve_at(g, "rinv"))
                    link(dve, ch, dve.tensor_tensor(yf, yf, rinv[:, :], ALU.mult))
                    for p in range(NPAIR):
                        ins = dve.tensor_scalar(yin[:, x, 0, p], yin[:, x, 0, p], cols[:, PC_LXG + p:PC_LXG + p + 1],
                                                cols[:, PC_LXB + p:PC_LXB + p + 1], ALU.mult, ALU.add)
                    link(dve, ch, ins)
                    link(dve, ch, dve.tensor_tensor(yin[:, x, 0], yin[:, x, 0], yin[:, x, 1], ALU.add))
                    dve.tensor_tensor(mix[:, NPAIR:, :], yin[:, x, 0], yin[:, x, 2], ALU.mult).then_inc(s_dve, 1)
                    for t in range(XT):
                        tile = bass.ds(g * XT + t, 1)
                        o = oin[:, x, t, :]
                        o3 = o.rearrange("p (h n) -> p h n", n=P)
                        link(dve, ch, dve.tensor_tensor(osq[:, :], o, o, ALU.mult))
                        dve.tensor_reduce(ost[:, 0, :], osq[:, :].rearrange("p (h n) -> p h n", n=P), AX, ALU.add)\
                            .then_inc(s_dve, 1)
                        dve.wait_ge(s_act, act_at(g, f"osd{t}"))
                        link(dve, ch, dve.reciprocal(ost[:, 1, :], ost[:, 1, :]))
                        link(dve, ch, dve.tensor_tensor(o3, o3, wide(ost[:, 1, :], P), ALU.mult))
                        dve.scalar_tensor_tensor(o3, o3, 1.0 - LAMBDA_INIT, middle(subln[:, :], H_A), ALU.mult, ALU.mult)\
                            .then_inc(s_dve, 1)
                        dve.wait_ge(s_pe, pe_at(g, f"proj{t}"))
                        dve.wait_ge(o_h[t], 16 * g + 16)
                        dve.tensor_tensor(hb[:, t, :], po[:, :, :].rearrange("p a n -> p (a n)"), xin[:, x, t, :], ALU.add)\
                            .then_inc(s_dve, 1)
                        dve.wait_ge(s_act, act_at(g, f"hsd{t}"))
                        dve.reciprocal(st[:, 2, t:t + 1], st[:, 1, t:t + 1]).then_inc(s_dve, 1)
                        dve.wait_ge(s_pe, pe_at(g, f"hT{t}"))
                        dve.tensor_tensor(tT[:, :, :], ph[:, :, :], wide(cols[:, PC_LN2:PC_LN2 + KC], P), ALU.mult)\
                            .then_inc(s_dve, 1)
                        dve.wait_ge(s_pe, pe_at(g, f"route{t}"))
                        link(dve, ch, dve.tensor_tensor(lg[:, :], pr[:, 0:4 + NE], b_rt[:, :], ALU.add))
                        dve.tensor_reduce(sm[:, 0:1], lg[:, 0:4], AX, ALU.max, negate=True).then_inc(s_dve, 1)
                        link(dve, ch, dve.tensor_copy(g8[:, 0:4], lg[:, 0:4]))
                        dve.sem_inc(s_apart, 1)
                        link(dve, ch, dve.max(m8[:, :], g8[:, :]))
                        dve.sem_inc(s_apart, 1)
                        link(dve, ch, dve.max_index(i8[:, :], m8[:, :], g8[:, :]))
                        link(dve, ch, dve.tensor_copy(gi[:, :], i8[:, 0:1]))
                        link(dve, ch, dve.tensor_scalar(pen[:, :], giota[:, :], gi[:, :], NEG, ALU.not_equal, ALU.mult))
                        link(dve, ch, dve.tensor_tensor(pen[:, :], pen[:, :], lg[:, 4:], ALU.add))
                        dve.sem_inc(s_apart, 1)
                        link(dve, ch, dve.max(v8[:, :], pen[:, :]))
                        dve.tensor_scalar(sm[:, 2:3], v8[:, 0:1], -1.0, None, ALU.mult).then_inc(s_dve, 1)
                        dve.sem_inc(s_apart, 1)
                        link(dve, ch, dve.max_index(j8[:, :], v8[:, :], pen[:, :]))
                        link(dve, ch, dve.tensor_copy(ji[:, :], j8[:, 0:2]))
                        for n in range(2):
                            dve.tensor_scalar(keep["hot"][:, tile, n, :].rearrange("p a n -> p (a n)"), eiota[:, :],
                                              ji[:, n:n + 1], None, ALU.is_equal)
                        dve.wait_ge(s_act, act_at(g, f"e2{t}"))
                        link(dve, ch, dve.tensor_scalar(sm[:, 4:5], sm[:, 3:4], 1.0, None, ALU.add))
                        link(dve, ch, dve.tensor_tensor(sm[:, 5:6], sm[:, 4:5], sm[:, 1:2], ALU.mult))
                        link(dve, ch, dve.reciprocal(sm[:, 6:7], sm[:, 5:6]))
                        link(dve, ch, dve.tensor_tensor(sm[:, 7:8], sm[:, 6:7], sm[:, 3:4], ALU.mult))
                        dve.tensor_copy(keep["gate"][:, tile, :].rearrange("p a n -> p (a n)"), sm[:, 6:8]).then_inc(s_dve, 1)
                    ch.end("merge, VectorE")


def dispatch(nc, io, dr, keep, ahead):
    with ExitStack() as ctx:
        m = Pool(nc, ctx, "ds")
        before = m.sb("before", [P, P])
        ones = m.sb("ones", [P, P])
        blocks = m.sb("blocks", [P, NT])
        picked = m.sb("picked", [P, NT, NE])
        dest = m.sb("dest", [P, NT, NE])
        total = m.sb("total", [P, NT, NE])
        base = m.sb("base", [P, NE])
        more = m.sb("more", [P, NE, NT])
        nb = m.sb("nb", [P, NE])
        ones_e = m.sb("ones_e", [P, NE])
        ends = m.sb("ends", [P, NE])
        nbi = m.sb("nbi", [P, 2, NE], I32)
        tmp = m.sb("tmp", [P, NT, NE])
        slotf = m.sb("slotf", [P, NT, 2])
        ids = m.sb("ids", [P, NT], I32)
        zero = m.sb("zero", [P, NB], I32)
        pr = m.ps("pr", [P, 512])
        pc = m.ps("pc", [P, 512])
        s_const = m.sem("const")
        s_ids = m.sem("ids_done")
        s_zero = m.sem("zero_done")
        s_picked = m.sem("picked_done")
        s_pe = m.sem("pe")
        s_ch = m.sem("chain")
        s_slots = m.sem("slots")
        o_sc = m.sem("o_sc")
        block = ctx.enter_context(nc.Block())

        @block.sync
        def _(sp):
            ahead(sp)
            for dst, src in ((before[:, :], io["c_before"]), (ones[:, :], io["c_ones"]), (blocks[:, :], io["c_blocks"])):
                sp.dma_start(dst, src).then_inc(s_const, 16)
            sp.wait_ge(s_zero, 1)
            sp.dma_start(dr["slot_tok"].rearrange("(p n) a -> p (n a)", p=P), zero[:, :]).then_inc(s_zero, 16)

        @block.gpsimd
        def _(pool):
            pool.memset(zero[:, :], 0).then_inc(s_zero, 1)
            pool.iota(ids[:, :], [[P, NT]], base=0, channel_multiplier=1).then_inc(s_ids, 1)
            pool.wait_ge(s_zero, 17)
            pool.wait_ge(s_slots, 1)
            pool.wait_ge(s_ids, 1)
            for t in range(NT):
                for n in range(2):
                    pool.indirect_dma_start(dr["slot_tok"], bass.IndirectOffsetOnAxis(keep["slot"][:, t, n:n + 1], 0),
                                            ids[:, t:t + 1], None).then_inc(o_sc, 16)
            pool.wait_ge(o_sc, 16 * 2 * NT)

        @block.tensor
        def _(pe):
            pe.wait_ge(s_const, 48)
            pe.wait_ge(s_picked, 1)
            flat = picked[:, :, :].rearrange("p a n -> p (a n)")
            pe.matmul(pr[:, :], before[:, :], flat, start=True, stop=True)
            pe.matmul(pc[:, :], ones[:, :], flat, start=True, stop=True).then_inc(s_pe, 1)

        @block.vector
        def _(dve):
            dve.tensor_tensor(picked[:, :, :], keep["hot"][:, :, 0, :], keep["hot"][:, :, 1, :], ALU.add).then_inc(s_picked, 1)
            n = [0]

            def chain(ins):
                n[0] += 1
                ins.then_inc(s_ch, 1)
                dve.wait_ge(s_ch, n[0])

            dve.wait_ge(s_const, 48)
            dve.wait_ge(s_pe, 1)
            chain(dve.tensor_copy(total[:, :, :].rearrange("p a n -> p (a n)"), pc[:, :]))
            dve.memset(ones_e[:, :], 1.0)
            chain(dve.memset(base[:, :], 0.0))
            for t in range(NT):
                dve.tensor_tensor(dest[:, t, :], pr[:, t * NE:(t + 1) * NE], base[:, :], ALU.add)
                chain(dve.tensor_tensor(base[:, :], base[:, :], total[:, t, :], ALU.add))
            chain(dve.tensor_tensor(more[:, :, :], wide(base[:, :], NT), middle(blocks[:, :], NE), ALU.is_gt))
            chain(dve.tensor_reduce(nb[:, :], more[:, :, :], AX, ALU.add))
            chain(dve.tensor_scalar(nb[:, :], nb[:, :], 1.0, None, ALU.add))
            chain(dve.tensor_tensor_scan(ends[:, :], ones_e[:, :], nb[:, :], 0.0, ALU.mult, ALU.add))
            dve.tensor_copy(nbi[:, 1, :], nb[:, :])
            chain(dve.tensor_tensor(ends[:, :], ends[:, :], nb[:, :], ALU.subtract))
            dve.tensor_copy(keep["blocks"][:, 0, :], nb[:, :])
            dve.tensor_copy(keep["blocks"][:, 1, :], ends[:, :])
            chain(dve.tensor_scalar(ends[:, :], ends[:, :], float(P), None, ALU.mult))
            chain(dve.tensor_tensor(dest[:, :, :], dest[:, :, :], middle(ends[:, :], NT), ALU.add))
            for k in range(2):
                chain(dve.tensor_tensor(tmp[:, :, :], dest[:, :, :], keep["hot"][:, :, k, :], ALU.mult))
                chain(dve.tensor_reduce(slotf[:, :, k], tmp[:, :, :], AX, ALU.add))
            dve.tensor_copy(keep["slot"][:, :, :], slotf[:, :, :]).then_inc(s_slots, 1)


def experts(nc, io, dr, keep):
    with ExitStack() as ctx:
        m = Pool(nc, ctx, "ex")
        wg = [m.sb(f"wg{x}", [P, KC, DE]) for x in range(2)]
        wu = [m.sb(f"wu{x}", [P, KC, DE]) for x in range(2)]
        wd = [m.sb(f"wd{x}", [P, DE // P, D]) for x in range(2)]
        s_w = [m.sem(f"w{x}") for x in range(2)]

        def weights(sp, e, x):
            for dst, src in ((wg[x], io["w_exp_gate"]), (wu[x], io["w_exp_up"]), (wd[x], io["w_exp_down"])):
                sp.dma_start(dst[:, :, :], src[0, e].rearrange("a (k p) n -> p (a k) n", p=P)).then_inc(s_w[x], 16)

        dispatch(nc, io, dr, keep, lambda sp: [weights(sp, bass.ds(x, 1), x) for x in range(2)])

        ident = m.sb("ident", [P, P])
        cols = m.sb("cols", [P, PC_N])
        idx = m.sb("idx", [P, 1], U32)
        xb = m.sb("xb", [P, D])
        xT = m.sb("xT", [P, KC, P])
        sg = m.sb("sg", [P, DE])
        hh = m.sb("hh", [P, DE])
        hT = m.sb("hT", [P, DE // P, P])
        yb = m.sb("yb", [P, D])
        px = m.ps("px", [P, KC, P])
        pg = m.ps("pg", [P, DE])
        pu = m.ps("pu", [P, DE])
        phT = m.ps("phT", [P, DE])
        py = m.ps("py", [P, 2, 512])
        s_const = m.sem("const")
        s_done = m.sem("done")
        s_idx = m.sem("idx_ld")
        s_x = m.sem("x")
        s_px = m.sem("px_done")
        s_xT = m.sem("xT_done")
        s_pg = m.sem("pg_done")
        s_pu = m.sem("pu_done")
        s_sg = m.sem("sg_done")
        s_hh = m.sem("hh_done")
        s_phT = m.sem("phT_done")
        s_hT = m.sem("hT_done")
        s_py = m.sem("py_done")
        s_yb = m.sem("yb_done")
        o_y = m.sem("o_y")
        s_apart = m.sem("apart")
        s_apart_pe = m.sem("apart_pe")
        block = ctx.enter_context(nc.Block())

        def turns(eng, body, before=None, past=None):
            with eng.Fori(0, NE // 2) as i:
                for x in range(2):
                    n = eng.value_load(keep["blocks"][0:1, 0, bass.ds(2 * i + x, 1)], min_val=1, max_val=NT)
                    first = eng.value_load(keep["blocks"][0:1, 1, bass.ds(2 * i + x, 1)], min_val=0, max_val=NB - 2)
                    if before:
                        before(i, x)
                    with eng.Fori(0, n) as j:
                        body(nc.s_assert_within(first + j, 0, NB - 2, skip_runtime_bounds_check_because="the experts' blocks add up to less than NB"), x)
                    if past:
                        past()

        @block.sync
        def _(sp):
            sp.dma_start(ident[:, :], io["c_ident"]).then_inc(s_const, 16)
            sp.dma_start(cols[:, :], io["cols"]).then_inc(s_const, 16)
            with sp.Fori(0, NE // 2 - 1) as i:
                for x in range(2):
                    sp.wait_ge(s_done, 2 * i + x + 1)
                    weights(sp, bass.ds(2 * i + x + 2, 1), x)

        @block.gpsimd
        def _(pool):
            def gather(b):
                pool.dma_start(idx[:, :], dr["slot_tok"][bass.ds(b * P, P), :]).then_inc(s_idx, 16)
                pool.wait_ge(s_idx, 16 * b + 16)
                pool.sem_inc(s_apart, 1)
                pool.indirect_dma_start(xb[:, :], None, dr["hn"], bass.IndirectOffsetOnAxis(idx[:, 0:1], 0))\
                    .then_inc(s_x, 16)

            def body(b, x):
                pool.wait_ge(s_px, b + 1)
                pool.sem_inc(s_apart, 1)
                gather(b + 1)

            gather(0)
            turns(pool, body)

        @block.tensor
        def _(pe):
            def transpose_x(ks):
                for k in ks:
                    ins = pe.transpose(px[:, k, :], xb[:, k * P:(k + 1) * P], ident[:, :])
                return ins

            def body(b, x):
                pe.wait_ge(s_xT, b + 1)
                pe.wait_ge(s_hh, b + 1)
                for out, w, done in ((pg, wg[x], s_pg), (pu, wu[x], s_pu)):
                    for k in range(KC):
                        ins = pe.matmul(out[:, :], xT[:, k, :], w[:, k, :], start=(k == 0), stop=(k == KC - 1))
                    ins.then_inc(done, 1)
                pe.wait_ge(s_x, 16 * b + 32)
                transpose_x(range(KC // 2))
                pe.wait_ge(s_hh, b + 2)
                pe.wait_ge(s_hT, b + 1)
                for k in range(DE // P):
                    ins = pe.transpose(phT[:, k * P:(k + 1) * P], hh[:, k * P:(k + 1) * P], ident[:, :])
                ins.then_inc(s_phT, 1)
                transpose_x(range(KC // 2, KC)).then_inc(s_px, 1)
                pe.wait_ge(s_hT, b + 2)
                pe.wait_ge(s_yb, b + 1)
                for n in range(2):
                    for k in range(DE // P):
                        ins = pe.matmul(py[:, n, :], hT[:, k, :], wd[x][:, k, 512 * n:512 * n + 512],
                                        start=(k == 0), stop=(k == DE // P - 1))
                ins.then_inc(s_py, 1)

            def before(i, x):
                pe.wait_ge(s_w[x], 48 * i + 48)
                pe.sem_inc(s_apart_pe, 1)

            pe.wait_ge(s_const, 32)
            pe.wait_ge(s_x, 16)
            transpose_x(range(KC)).then_inc(s_px, 1)
            turns(pe, body, before)

        @block.scalar
        def _(act):
            def body(b, x):
                act.wait_ge(s_pg, b + 1)
                act.activation(sg[:, :], pg[:, :], ACT.Silu).then_inc(s_sg, 1)
                act.wait_ge(s_phT, b + 1)
                act.activation(hT[:, :, :].rearrange("p a n -> p (a n)"), phT[:, :], ACT.Copy).then_inc(s_hT, 1)
                act.wait_ge(s_py, b + 1)
                act.wait_ge(o_y, 16 * b + 16)
                act.activation(yb[:, :], py[:, :, :].rearrange("p a n -> p (a n)"), ACT.Copy).then_inc(s_yb, 1)
                act.wait_ge(s_yb, b + 2)
                act.dma_start(dr["slots"][bass.ds(b * P, P), :], yb[:, :]).then_inc(o_y, 16)

            act.sem_inc(s_hT, 1)
            act.sem_inc(s_yb, 1)
            act.sem_inc(o_y, 16)
            turns(act, body, past=lambda: act.sem_inc(s_done, 1))
            last = act.value_load(keep["blocks"][0:1, 1, NE - 1:NE], min_val=0, max_val=NB - 2)
            n = act.value_load(keep["blocks"][0:1, 0, NE - 1:NE], min_val=1, max_val=NT)
            act.wait_ge(o_y, 16 * last + 16 * n + 16)
            act.sem_inc(s_const, 1)

        @block.vector
        def _(dve):
            def copy_x(b):
                dve.tensor_tensor(xT[:, :, :], px[:, :, :], wide(cols[:, PC_LN2:PC_LN2 + KC], P), ALU.mult).then_inc(s_xT, 1)

            def body(b, x):
                dve.wait_ge(s_sg, b + 1)
                dve.wait_ge(s_pu, b + 1)
                dve.tensor_tensor(hh[:, :], sg[:, :], pu[:, :], ALU.mult).then_inc(s_hh, 1)
                dve.wait_ge(s_px, b + 2)
                copy_x(b + 1)

            dve.sem_inc(s_hh, 1)
            dve.wait_ge(s_const, 32)
            dve.wait_ge(s_px, 1)
            copy_x(0)
            turns(dve, body)

    with ExitStack() as ctx:
        m = Pool(nc, ctx, "cb")
        ya = [m.sb(f"ya{x}", [P, 2, D]) for x in range(2)]
        hb = [m.sb(f"hb{x}", [P, D]) for x in range(2)]
        acc = [m.sb(f"acc{x}", [P, D]) for x in range(2)]
        s_y = [m.sem(f"y{x}") for x in range(2)]
        s_h = [m.sem(f"h{x}") for x in range(2)]
        s_acc = m.sem("acc_done")
        s_ch = m.sem("chain")
        o_out = [m.sem(f"o_out{x}") for x in range(2)]
        block = ctx.enter_context(nc.Block())

        @block.gpsimd
        def _(pool):
            for t in range(NT):
                if t >= 2:
                    pool.wait_ge(s_acc, t - 1)
                for n in range(2):
                    pool.indirect_dma_start(ya[t % 2][:, n, :], None, dr["slots"],
                                            bass.IndirectOffsetOnAxis(keep["slot"][:, t, n:n + 1], 0)).then_inc(s_y[t % 2], 16)

        @block.sync
        def _(sp):
            for t in range(NT):
                if t >= 2:
                    sp.wait_ge(s_acc, t - 1)
                sp.dma_start(hb[t % 2][:, :], dr["h"][t * P:(t + 1) * P, :]).then_inc(s_h[t % 2], 16)

        @block.scalar
        def _(act):
            for t in range(NT):
                act.wait_ge(s_acc, t + 1)
                act.dma_start(io["out"][0, t * P:(t + 1) * P, :], acc[t % 2][:, :]).then_inc(o_out[t % 2], 16)
            for x in range(2):
                act.wait_ge(o_out[x], 16 * NT // 2)

        @block.vector
        def _(dve):
            for t in range(NT):
                x = t % 2
                dve.wait_ge(s_y[x], 32 * (t // 2) + 32)
                dve.wait_ge(s_h[x], 16 * (t // 2) + 16)
                dve.scalar_tensor_tensor(hb[x][:, :], ya[x][:, 0, :], keep["gate"][:, t, 0:1], hb[x][:, :],
                                         ALU.mult, ALU.add).then_inc(s_ch, 1)
                dve.wait_ge(s_ch, t + 1)
                if t >= 2:
                    dve.wait_ge(o_out[x], 16 * (t // 2))
                dve.scalar_tensor_tensor(acc[x][:, :], ya[x][:, 1, :], keep["gate"][:, t, 1:2], hb[x][:, :],
                                         ALU.mult, ALU.add).then_inc(s_acc, 1)


def build(nc, io, out):
    def scratch(name, shape, dt=F32):
        return nc.dram_tensor(name, shape, dt).ap()

    dr = {
        "qk": scratch("qk_s", [8, P, S]), "v": scratch("v_s", [S, DA]),
        "chunks": scratch("chunks_s", [NCH, P, NPAIR, ROW]),
        "o": scratch("o_s", [S, DA]), "y": scratch("y_s", [NPAIR, P, S]),
        "h": scratch("h_s", [S, D]), "hn": scratch("hn_s", [S, D]),
        "slot_tok": scratch("slot_tok_s", [NB * P, 1], I32), "slots": scratch("slots_s", [NB * P, D]),
        "bonus": scratch("bonus_s", [NPAIR, P, S]), "g": scratch("g_s", [NPAIR, P, S]),
    }
    io["out"] = out
    with ExitStack() as ctx:
        m = Pool(nc, ctx, "keep")
        keep = {
            "hot": m.sb("hot", [P, NT, 2, NE]),
            "gate": m.sb("gate", [P, NT, 2]),
            "slot": m.sb("slot", [P, NT, 2], U32),
            "blocks": m.sb("blocks", [P, 2, NE], I32),
        }
        project(nc, io, dr)
        attend(nc, io, dr)
        recur(nc, io, dr)
        merge(nc, io, dr, keep)
        experts(nc, io, dr, keep)


def constants():
    half = 8
    inv = np.float32(500000.0) ** (-np.arange(0, 16, 2, dtype=np.float32) / np.float32(16))
    ang = (np.arange(S, dtype=np.float32)[:, None] * inv[None, :].astype(np.float32)).astype(np.float32)
    cos, sin = np.cos(ang).T, np.sin(ang).T
    cosin = np.zeros((P, 2, S), np.float32)
    cosin[:, 0] = 1.0
    swap = np.zeros((P, P), np.float32)
    for b in (0, 64):
        cosin[b:b + half, 0] = cosin[b + half:b + 2 * half, 0] = cos
        cosin[b:b + half, 1] = -sin
        cosin[b + half:b + 2 * half, 1] = sin
        for i in range(half):
            swap[b + i, b + half + i] = swap[b + half + i, b + i] = 1.0
    ones2 = np.kron(np.eye(2), np.ones((64, 64))).astype(np.float32)
    mask = np.zeros((P, 2, P), np.float32)
    mask[0, 0, 0:C] = -1e30
    mask[0, 1, C:] = 1.0
    row, col = np.arange(P)[:, None] % C, np.arange(C)[None, :]
    one = lambda a: a.astype(np.float32)
    past = one(row <= col)
    mgb = np.concatenate([one((row < col) & (row // 16 == col // 16)), past], 1)
    mgk = np.concatenate([one(row < col), past], 1)
    mgl = np.stack([one((col < row) & (row // 16 == col // 16)),
                    one((row // 32 == col // 32) & (row // 16 > col // 16)), one(row // 32 > col // 32)], 1)
    reset = np.ones((P, GT), np.float32)
    reset[:, ::C] = 0.0
    return {"c_ident": np.eye(P, dtype=np.float32), "c_ones2": ones2, "c_swap": swap, "c_cosin": cosin,
            "c_reset": reset, "c_mean2": ones2 / 64,
            "c_giota": np.ascontiguousarray(np.broadcast_to(np.arange(NE, dtype=np.float32) // EPG, (P, NE))),
            "c_eiota": np.ascontiguousarray(np.broadcast_to(np.arange(NE, dtype=np.float32), (P, NE))),
            "c_before": np.triu(np.ones((P, P), np.float32), 1), "c_ones": np.ones((P, P), np.float32),
            "c_blocks": np.ascontiguousarray(np.broadcast_to(P * np.arange(1, NT + 1, dtype=np.float32), (P, NT))),
             "c_mask": mask,
            "c_eye": one(row == col), "c_mgb": mgb, "c_mgk": mgk, "c_mgl": mgl}


def kernel(**inputs):
    import concourse.bacc as _bacc
    from concourse.bass_utils import run_bass_kernel_spmd as _run

    def col(name):
        a = np.asarray(inputs[name])[0]
        return a.reshape(-1, P).T

    arrays = {n: np.ascontiguousarray(inputs[n]) for n in
              ("w_in", "w_lora_up", "a_lora_up", "g_lora_up", "w_out", "w_exp_gate", "w_exp_up", "w_exp_down")}
    x = np.asarray(inputs["x"])[0]
    arrays["x"] = np.concatenate([x, np.zeros((GT, D), x.dtype)])
    twice = lambda n: np.concatenate([np.asarray(inputs[n])[0]] * 2).reshape(P, 1)
    arrays["cols"] = np.ascontiguousarray(np.concatenate(
        [col(n) for n in ("ln1_g", "shift_mu", "w0", "a0", "k_k", "k_a", "r_k", "ln_x_g", "ln_x_b", "ln2_g")]
        + [twice("q_norm_g"), twice("k_norm_g")], axis=1))
    both = np.concatenate([np.asarray(inputs["w_router_group"])[0], np.asarray(inputs["w_router_expert"])[0]], 1)
    arrays["w_rt"] = np.ascontiguousarray(both.reshape(KC, P, 4 + NE).transpose(1, 0, 2))
    both = np.concatenate([np.asarray(inputs["b_router_group"])[0], np.asarray(inputs["b_router_expert"])[0]])
    arrays["b_rt"] = np.ascontiguousarray(np.broadcast_to(both, (P, 4 + NE)))
    arrays["subln"] = np.ascontiguousarray(np.broadcast_to(np.asarray(inputs["subln_g"])[0], (P, P)))
    lams = np.stack([np.asarray(inputs[n])[0] for n in ("lambda_q1", "lambda_k1", "lambda_q2", "lambda_k2")])
    arrays["lams"] = np.ascontiguousarray(np.broadcast_to(lams, (P, 4, 64)))
    arrays.update(constants())
    nc = _bacc.Bacc("TRN2", target_bir_lowering=False, num_devices=1)
    io = {n: nc.dram_tensor(f"in_{n}", a.shape, mybir.dt.from_np(a.dtype), kind="ExternalInput").ap()
          for n, a in arrays.items()}
    out = nc.dram_tensor("out_0", (1, S, D), F32, kind="ExternalOutput").ap()
    build(nc, io, out)
    r = _run(nc, [{f"in_{n}": a for n, a in arrays.items()}], core_ids=[0])
    return r.results[0]["out_0"]
```

```python
from contextlib import ExitStack

import concourse.bass as bass
from concourse import mybir
import numpy as np

F32 = mybir.dt.float32
I32 = mybir.dt.int32
U32 = mybir.dt.uint32
ACT = mybir.ActivationFunctionType
ALU = mybir.AluOpType
AX = mybir.AxisListType.X

P = 128
D = 1024
S = 2048
KC = D // P
GT = 256
NG = S // GT
NT = S // P
DA = 512
H_A = 4
RW = 1792
RT = RW // P
NPAIR = 4
C = 64
NCH = S // C
CPG = GT // C
ROW = 5 * C + 1
N_IN = 3 * DA + RW
NE = 32
EPG = 8
DE = 512
NB = 2 * S // P + NE
E_HALF = float(np.exp(-0.5))
LAMBDA_INIT = 0.8 - 0.6 * float(np.exp(-0.3 * 0))

PC_LN1, PC_MU, PC_W0, PC_A0, PC_KK, PC_KA, PC_RK, PC_LXG, PC_LXB, PC_LN2, PC_QG, PC_KG = (
    0, 8, 22, 26, 30, 34, 38, 42, 46, 50, 58, 59)
PC_N = 60


class Pool:

    def __init__(self, nc, ctx, tag):
        self.nc, self.ctx, self.tag = nc, ctx, tag

    def sb(self, name, shape, dt=F32):
        return self.ctx.enter_context(self.nc.sbuf_tensor(f"{self.tag}_{name}", shape, dt))

    def ps(self, name, shape, dt=F32):
        return self.ctx.enter_context(self.nc.psum_tensor(f"{self.tag}_{name}", shape, dt))

    def sem(self, name):
        return self.ctx.enter_context(self.nc.semaphore(f"{self.tag}_{name}"))


class Count:

    def __init__(self, sem, turn, per):
        self.sem, self.turn, self.per, self.n = sem, turn, per, 0

    def at(self, n):
        return self.turn * self.per + n

    def step(self, ins):
        self.n += 1
        ins.then_inc(self.sem, 1)

    def end(self, what):
        assert self.n == self.per, (what, self.n, self.per)


def link(eng, count, ins):
    count.step(ins)
    eng.wait_ge(count.sem, count.at(count.n))


def wide(ap, n):
    return ap.unsqueeze(2).broadcast_to([ap.shape[0], ap.shape[1], n])


def middle(ap, n):
    return ap.unsqueeze(1).broadcast_to([ap.shape[0], n, ap.shape[1]])


MAIN = [("mix", 12), ("mix", 13)]
for _p in range(NPAIR):
    MAIN += [("mix", 4 + _p), ("mix", _p), ("mix", 8 + _p)]
MAIN += [("v", 0)] + [("qk", _i) for _i in range(8)] + [("v", 1)]
NM = len(MAIN)
AUX_A = {j: [] for j in range(NM)}
AUX_D = {j: [] for j in range(NM)}
for _p in range(NPAIR):
    AUX_A[3 + 3 * _p] += [("g", _p)]
    AUX_A[4 + 3 * _p] += [("w", _p), ("a", _p)]
    AUX_A[6 + 3 * _p] += [("kk", _p)]
    AUX_D[7 + 3 * _p] += [("bonus", _p)]
for _i in range(8):
    AUX_A[16 + _i] += [("norm", _i)]
    AUX_D[min(17 + _i, NM - 1)] += [("turn", _i)]
ORDER_A = [x for j in range(NM) for x in AUX_A[j]]
ORDER_D = [x for j in range(NM) for x in AUX_D[j]]
NA, ND = len(ORDER_A), len(ORDER_D)
X_SQUARE, X_SCALE, X_TURN = {17: 0, 20: 1}, {18: 0, 21: 1}, {19: 0, 22: 1}
XT = GT // P


def project(nc, io, dr):
    with ExitStack() as ctx:
        m = Pool(nc, ctx, "pj")
        w_in = m.sb("w_in", [P, KC, N_IN])
        xnT = m.sb("xnT", [P, 2, KC, GT])
        xt = m.sb("xt", [P, XT, D])
        junk = m.sb("junk", [P, D])
        ident = m.sb("ident", [P, P])
        ones2 = m.sb("ones2", [P, P])
        swap = m.sb("swap", [P, P])
        cols = m.sb("cols", [P, PC_N])
        ncol = m.sb("ncol", [P, 14])
        loras = m.sb("loras", [P, 2, DA])
        cosin = m.sb("cosin", [P, 2, GT])
        reset = m.sb("reset", [P, GT])
        stat = m.sb("stat", [P, 3, XT])
        eps = m.sb("eps", [P, 1])
        carry = m.sb("carry", [P, RT])
        ubuf = m.sb("ubuf", [P, 2, GT])
        lo = m.sb("lo", [P, 2, GT])
        lot = m.sb("lot", [P, 2, GT])
        krv = m.sb("krv", [P, 2, 3, GT])
        za = m.sb("za", [P, 2, GT])
        cz = m.sb("cz", [P, GT])
        dec = m.sb("dec", [P, 3, GT])
        gout = m.sb("gout", [P, GT])
        kk = m.sb("kk", [P, 2, GT])
        ksq = m.sb("ksq", [P, GT])
        kn = m.sb("kn", [P, GT])
        kmod = m.sb("kmod", [P, GT])
        rk = m.sb("rk", [P, GT])
        bon = m.sb("bon", [P, GT])
        st = m.sb("st", [P, CPG, ROW])
        qr = m.sb("qr", [P, 2, GT])
        qsq = m.sb("qsq", [P, 2, GT])
        qrr = m.sb("qrr", [P, 2, GT])
        qn = m.sb("qn", [P, 2, GT])
        m1 = m.sb("m1", [P, GT])
        m2 = m.sb("m2", [P, GT])
        qo = m.sb("qo", [P, GT])
        vo = m.sb("vo", [P, DA])

        tp = m.ps("tp", [P, KC, P])
        big = [m.ps(f"big{i}", [P, 512]) for i in range(2)]
        aux_a = [m.ps(f"aux_a{i}", [P, 512]) for i in range(2)]
        aux_d = [m.ps(f"aux_d{i}", [P, 512]) for i in range(2)]

        s_const = m.sem("const")
        s_wqkv = m.sem("wqkv")
        s_ncol = m.sem("ncol")
        s_x = [m.sem(f"x{i}") for i in range(XT)]
        s_cs = m.sem("cs")
        s_rms = m.sem("rms")
        s_rstd = m.sem("rstd")
        s_xs = m.sem("xs")
        s_tp = m.sem("tp_done")
        s_xnT = m.sem("xnT_done")
        s_main = m.sem("main")
        s_evac = m.sem("evac")
        s_mixed = m.sem("mixed")
        s_tanh = m.sem("tanh")
        s_eg = m.sem("eg")
        s_sig = m.sem("sig")
        s_kk0 = m.sem("kk0")
        s_ksq = m.sem("ksq_done")
        s_scan = m.sem("scan")
        s_dec = m.sem("dec_done")
        s_rk = m.sem("rk_done")
        s_prep = m.sem("prep")
        s_qn = m.sem("qn_done")
        s_qo = m.sem("qo_done")
        s_aa = m.sem("aa")
        s_aa_free = m.sem("aa_free")
        s_ad = m.sem("ad")
        s_ad_free = m.sem("ad_free")
        s_act = m.sem("act")
        s_dve = m.sem("dve")
        o_st, o_bon, o_g, o_q, o_v = (m.sem(n) for n in ("o_st", "o_bon", "o_g", "o_q", "o_v"))
        block = ctx.enter_context(nc.Block())

        w_v = io["w_in"][0].rearrange("(k p) n -> p k n", p=P)
        consts = [(ident[:, :], io["c_ident"]), (ones2[:, :], io["c_ones2"]), (swap[:, :], io["c_swap"]),
                  (cols[:, :], io["cols"]), (reset[:, :], io["c_reset"]),
                  (loras[0:64, 0, :], io["w_lora_up"][0]), (loras[64:128, 0, :], io["a_lora_up"][0]),
                  (loras[:, 1, :], io["g_lora_up"][0]),
                  (w_in[:, :, 3 * DA:], w_v[:, :, 3 * DA:])]
        N_CONST = 16 * len(consts)

        @block.sync
        def _(sp):
            for t in range(XT):
                sp.dma_start(xt[:, t, :], io["x"][t * P:(t + 1) * P, :]).then_inc(s_x[t], 16)
            for dst, src in consts:
                sp.dma_start(dst, src).then_inc(s_const, 16)
            sp.dma_start(w_in[:, :, 0:3 * DA], w_v[:, :, 0:3 * DA]).then_inc(s_wqkv, 16)
            for t in range(XT):
                sp.wait_ge(s_tp, t + 1)
                sp.dma_start(xt[:, t, :], io["x"][GT + t * P:GT + (t + 1) * P, :]).then_inc(s_x[t], 16)
            with sp.Fori(0, NG) as g:
                sp.wait_ge(s_qo, 8 * g + 1)
                sp.dma_start(cosin[:, :, :], io["c_cosin"][:, :, bass.ds(g * GT, GT)]).then_inc(s_cs, 16)
                for j, (kind, i) in enumerate(MAIN):
                    if j in X_TURN:
                        t = X_TURN[j]
                        sp.wait_ge(s_tp, XT * (g + 1) + t + 1)
                        sp.dma_start(xt[:, t, :], io["x"][bass.ds(g * GT + 2 * GT + t * P, P), :]).then_inc(s_x[t], 16)
                    for what, p in AUX_A[j]:
                        if what == "g":
                            sp.wait_ge(s_aa_free, NA * g + ORDER_A.index((what, p)) + 3)
                            sp.dma_start(dr["g"][p, :, bass.ds(g * GT, GT)], gout[:, :]).then_inc(o_g, 16)
                        if what == "kk":
                            sp.wait_ge(s_prep, 4 * g + p + 2)
                            sp.dma_start(dr["chunks"][bass.ds(g * CPG, CPG), :, p, :].rearrange("c p n -> p c n"),
                                         st[:, :, :]).then_inc(o_st, 16)
                    for what, p in AUX_D[j]:
                        if what == "bonus":
                            sp.wait_ge(s_ad_free, ND * g + ORDER_D.index((what, p)) + 3)
                            sp.dma_start(dr["bonus"][p, :, bass.ds(g * GT, GT)], bon[:, :]).then_inc(o_bon, 16)
                        if what == "turn":
                            sp.wait_ge(s_qo, 8 * g + p + 2)
                            sp.dma_start(dr["qk"][p, :, bass.ds(g * GT, GT)], qo[:, :]).then_inc(o_q, 16)
                    if kind == "v":
                        sp.wait_ge(s_evac, NM * g + j + 3)
                        sp.dma_start(dr["v"][bass.ds(g * GT + i * P, P), :], vo[:, :]).then_inc(o_v, 16)
            for sem, n in ((o_g, 4), (o_st, 4), (o_bon, 4), (o_q, 8), (o_v, XT)):
                sp.wait_ge(sem, 16 * n * NG + 16)
            for t in range(XT):
                sp.wait_ge(s_x[t], 16 * NG + 32)

        @block.tensor
        def _(pe):
            pe.wait_ge(s_const, N_CONST)
            pe.wait_ge(s_ncol, 1)
            pe.sem_inc(s_main, 1)
            def transpose_x(g, t):
                pe.wait_ge(s_xs, XT * g + t + 1)
                pe.wait_ge(s_xnT, XT * g + t + 1)
                for k in range(KC):
                    ins = pe.transpose(tp[:, k, :], xt[:, t, k * P:(k + 1) * P], ident[:, :])
                ins.then_inc(s_tp, 1)

            def group(g, half):
                pe.wait_ge(s_xnT, XT * g + XT + 1)
                na = nd = 0
                for j, (kind, i) in enumerate(MAIN):
                    pe.wait_ge(s_evac, NM * g + j + 1)
                    if kind != "mix" and MAIN[j - 1][0] == "mix":
                        pe.wait_ge(s_wqkv, 16)
                    for k in range(KC):
                        if kind == "v":
                            out, lhs, rhs = big[j % 2][:, 0:DA], xnT[:, half, k, i * P:(i + 1) * P], w_in[:, k, 2 * DA:3 * DA]
                        else:
                            c0 = 3 * DA + i * P if kind == "mix" else i * P
                            out, lhs, rhs = big[j % 2][:, 0:GT], w_in[:, k, c0:c0 + P], xnT[:, half, k, :]
                        ins = pe.matmul(out, lhs, rhs, start=(k == 0), stop=(k == KC - 1))
                    ins.then_inc(s_main, 1)
                    if j in X_TURN:
                        transpose_x(g + 1, X_TURN[j])
                    for what, p in AUX_A[j]:
                        pe.wait_ge(s_aa_free, NA * g + na + 1)
                        out = aux_a[na % 2][:, 0:GT]
                        cs = slice(p * P, (p + 1) * P)
                        if what == "w":
                            pe.wait_ge(s_tanh, g + 1)
                            lhs, rhs = loras[0:64, 0, cs], lot[0:64, 0, :]
                        elif what == "a":
                            pe.wait_ge(s_mixed, RT * g + 3)
                            lhs, rhs = loras[64:128, 0, cs], lo[64:128, 0, :]
                        elif what == "g":
                            pe.wait_ge(s_sig, g + 1)
                            lhs, rhs = loras[:, 1, cs], lot[:, 1, :]
                        elif what == "kk":
                            pe.wait_ge(s_ksq, 4 * g + p + 1)
                            lhs, rhs = ones2[:, :], ksq[:, :]
                        else:
                            pe.wait_ge(s_evac, NM * g + 15 + p + 3)
                            lhs, rhs = ones2[:, :], qsq[:, p % 2, :]
                        pe.matmul(out, lhs, rhs, start=True, stop=True).then_inc(s_aa, 1)
                        na += 1
                    for what, p in AUX_D[j]:
                        pe.wait_ge(s_ad_free, ND * g + nd + 1)
                        if what == "bonus":
                            pe.wait_ge(s_rk, 4 * g + p + 1)
                            lhs, rhs = ones2[:, :], rk[:, :]
                        else:
                            pe.wait_ge(s_qn, 8 * g + p + 3)
                            lhs, rhs = swap[:, :], qn[:, p % 2, :]
                        pe.matmul(aux_d[nd % 2][:, 0:GT], lhs, rhs, start=True, stop=True).then_inc(s_ad, 1)
                        nd += 1

            for t in range(XT):
                transpose_x(0, t)
            with pe.Fori(0, NG // 2) as i2:
                for half in range(2):
                    group(2 * i2 + half, half)

        @block.scalar
        def _(act):
            act.sem_inc(s_evac, 2)
            act.sem_inc(s_aa_free, 2)
            act.sem_inc(o_g, 16)
            act.sem_inc(o_v, 16)
            act.wait_ge(s_const, N_CONST)
            act.wait_ge(s_ncol, 1)

            def square_x(ch, g, t):
                act.wait_ge(s_x[t], 16 * g + 16)
                link(act, ch, act.activation(junk[:, :], xt[:, t, :], ACT.Square, accum_out=stat[:, 0, t:t + 1]))
                act.activation(stat[:, 1, t:t + 1], stat[:, 0, t:t + 1], ACT.Sqrt, bias=eps[:, :],
                               scale=1.0 / D).then_inc(s_rms, 1)

            def scale_x(g, t):
                act.wait_ge(s_rstd, XT * g + t + 1)
                act.activation(xt[:, t, :], xt[:, t, :], ACT.Copy, scale=stat[:, 2, t:t + 1]).then_inc(s_xs, 1)

            ch = Count(s_act, 0, XT)
            for t in range(XT):
                square_x(ch, 0, t)
                scale_x(0, t)
            with act.Fori(0, NG) as g:
                ch = Count(s_act, g + 1, XT)
                na = 0
                for j, (kind, i) in enumerate(MAIN):
                    act.wait_ge(s_main, NM * g + j + 2)
                    if kind == "mix":
                        act.wait_ge(s_mixed, RT * g + j + 1)
                        act.activation(ubuf[:, j % 2, :], big[j % 2][:, 0:GT], ACT.Copy).then_inc(s_evac, 1)
                    elif kind == "qk":
                        act.wait_ge(s_qn, 8 * g + i + 1)
                        act.activation(qr[:, i % 2, :], big[j % 2][:, 0:GT], ACT.Copy)
                        act.activation(qsq[:, i % 2, :], big[j % 2][:, 0:GT], ACT.Square).then_inc(s_evac, 1)
                    else:
                        act.wait_ge(o_v, 16 * XT * g + 16 * i + 16)
                        act.activation(vo[:, :], big[j % 2][:, 0:DA], ACT.Copy).then_inc(s_evac, 1)
                    if j in X_SQUARE:
                        square_x(ch, g + 1, X_SQUARE[j])
                    if j in X_SCALE:
                        scale_x(g + 1, X_SCALE[j])
                    if j == 0:
                        act.wait_ge(s_mixed, RT * g + 3)
                        act.activation(lot[0:64, 0, :], lo[0:64, 0, :], ACT.Tanh).then_inc(s_tanh, 1)
                    if j == 1:
                        act.wait_ge(s_mixed, RT * g + 4)
                        act.activation(lot[:, 1, :], lo[:, 1, :], ACT.Tanh, scale=0.5).then_inc(s_eg, 1)
                    if j < 14 and j % 3 == 1 and j >= 4:
                        act.wait_ge(s_kk0, 4 * g + (j - 4) // 3 + 1)
                        act.activation(ksq[:, :], kk[:, (j - 4) // 3 % 2, :], ACT.Square).then_inc(s_ksq, 1)
                    if 5 <= j <= 14 and j % 3 == 2:
                        p = (j - 5) // 3
                        act.wait_ge(s_scan, 4 * g + p + 1)
                        act.activation(dec[:, 0, :], cz[:, :], ACT.Exp, scale=-E_HALF)
                        act.activation(dec[:, 1, :], za[:, 0, :], ACT.Exp, scale=-E_HALF)
                        act.activation(dec[:, 2, :], cz[:, :], ACT.Exp, scale=E_HALF).then_inc(s_dec, 1)
                    for what, p in AUX_A[j]:
                        act.wait_ge(s_aa, NA * g + na + 1)
                        src = aux_a[na % 2][:, 0:GT]
                        if what == "w":
                            act.wait_ge(s_prep, 4 * g + p + 1)
                            ins = act.activation(za[:, 0, :], src, ACT.Tanh, bias=ncol[:, p:p + 1], scale=0.5)
                        elif what == "a":
                            ins = act.activation(za[:, 1, :], src, ACT.Tanh, bias=ncol[:, 4 + p:5 + p], scale=0.5)
                        elif what == "g":
                            act.wait_ge(o_g, 64 * g + 16 * p + 16)
                            ins = act.activation(gout[:, :], src, ACT.Copy)
                        elif what == "kk":
                            ins = act.activation(kn[:, :], src, ACT.Sqrt)
                        else:
                            ins = act.activation(qrr[:, p % 2, :], src, ACT.Sqrt, bias=eps[:, :], scale=1.0 / 64)
                        ins.then_inc(s_aa_free, 1)
                        na += 1
                ch.end("project, ScalarE")

        @block.vector
        def _(dve):
            for sem, n in ((s_xnT, 1), (s_mixed, 2), (s_prep, 1), (s_qn, 2), (s_qo, 1), (s_ad_free, 2),
                           (o_st, 16), (o_bon, 16), (o_q, 16)):
                dve.sem_inc(sem, n)
            dve.memset(carry[:, :], 0.0)
            dve.memset(eps[:, :], 1e-6)
            dve.wait_ge(s_const, N_CONST)
            dve.tensor_scalar(ncol[:, 0:8], cols[:, PC_W0:PC_W0 + 8], 0.5, None, ALU.mult)
            dve.tensor_scalar(ncol[:, 12:13], cols[:, PC_QG:PC_QG + 1], 0.125, None, ALU.mult)
            dve.tensor_copy(ncol[:, 13:14], cols[:, PC_KG:PC_KG + 1])
            dve.tensor_scalar(ncol[:, 8:12], cols[:, PC_KA:PC_KA + 4], -1.0, 1.0, ALU.mult, ALU.add).then_inc(s_ncol, 1)
            dve.wait_ge(s_ncol, 1)
            def invert_rms(g, t):
                dve.wait_ge(s_rms, XT * g + t + 1)
                dve.reciprocal(stat[:, 2, t:t + 1], stat[:, 1, t:t + 1]).then_inc(s_rstd, 1)

            def scale_xT(g, half, t):
                dve.wait_ge(s_tp, XT * g + t + 1)
                dve.tensor_tensor(xnT[:, half, :, t * P:(t + 1) * P], tp[:, :, :],
                                  wide(cols[:, PC_LN1:PC_LN1 + KC], P), ALU.mult).then_inc(s_xnT, 1)

            def group(g, half):
                ch = Count(s_dve, g, 2 * RT - 14 + 4 * 7 + 8 * 2)

                def chunked(ap):
                    return ap.rearrange("p (c n) -> p c n", n=C)

                nd = 0
                for j, (kind, i) in enumerate(MAIN):
                    if j in X_SQUARE:
                        invert_rms(g + 1, X_SQUARE[j])
                    if j in X_TURN:
                        scale_xT(g + 1, 1 - half, X_TURN[j])
                    if kind == "mix":
                        u = ubuf[:, j % 2, :]
                        if j < 2:
                            dst = lo[:, j, :]
                        else:
                            dst = krv[:, (j - 2) // 3 % 2, (j - 2) % 3, :]
                        dve.wait_ge(s_evac, NM * g + j + 3)
                        dve.tensor_tensor(dst[:, 1:], u[:, 0:GT - 1], u[:, 1:], ALU.subtract)
                        link(dve, ch, dve.tensor_tensor(dst[:, 0:1], carry[:, i:i + 1], u[:, 0:1], ALU.subtract))
                        dve.tensor_copy(carry[:, i:i + 1], u[:, GT - 1:GT])
                        dve.scalar_tensor_tensor(dst, dst, cols[:, PC_MU + i:PC_MU + i + 1], u,
                                                 ALU.mult, ALU.add).then_inc(s_mixed, 1)
                        if j == 1:
                            dve.wait_ge(s_eg, g + 1)
                            dve.tensor_scalar(lot[:, 1, :], lot[:, 1, :], 0.5, 0.5, ALU.mult, ALU.add).then_inc(s_sig, 1)
                        if j >= 2 and (j - 2) % 3 == 0:
                            p = (j - 2) // 3
                            dve.wait_ge(s_mixed, RT * g + j + 3)
                            dve.tensor_scalar(kk[:, p % 2, :], dst, cols[:, PC_KK + p:PC_KK + p + 1], None,
                                              ALU.mult).then_inc(s_kk0, 1)
                    for what, p in AUX_A[j]:
                        ready = NA * g + ORDER_A.index((what, p)) + 3
                        if what == "kk":
                            k, r, v = (krv[:, p % 2, n, :] for n in range(3))
                            dve.wait_ge(s_aa_free, ready)
                            link(dve, ch, dve.tensor_scalar(kn[:, :], kn[:, :], 1e-12, None, ALU.max))
                            link(dve, ch, dve.reciprocal(kn[:, :], kn[:, :]))
                            link(dve, ch, dve.tensor_tensor(kk[:, p % 2, :], kk[:, p % 2, :], kn[:, :], ALU.mult))
                            dve.wait_ge(s_dec, 4 * g + p + 1)
                            dve.wait_ge(o_st, 64 * g + 16 * p + 16)
                            link(dve, ch, dve.tensor_tensor(za[:, 1, :], kk[:, p % 2, :], za[:, 1, :], ALU.mult))
                            dve.scalar_tensor_tensor(st[:, :, 0:C], chunked(kk[:, p % 2, :]), -1.0,
                                                     chunked(dec[:, 1, :]), ALU.mult, ALU.mult)
                            dve.tensor_tensor(st[:, :, C:2 * C], chunked(r), chunked(dec[:, 0, :]), ALU.mult)
                            dve.tensor_tensor(st[:, :, 2 * C:3 * C], chunked(za[:, 1, :]), chunked(dec[:, 2, :]), ALU.mult)
                            dve.tensor_tensor(st[:, :, 3 * C:4 * C], chunked(kmod[:, :]), chunked(dec[:, 2, :]), ALU.mult)
                            dve.tensor_copy(st[:, :, 4 * C:5 * C], chunked(v))
                            dve.tensor_copy(st[:, :, 5 * C:5 * C + 1], chunked(dec[:, 0, :])[:, :, C - 1:C]).then_inc(s_prep, 1)
                        if what == "norm":
                            dve.wait_ge(s_aa_free, ready)
                            link(dve, ch, dve.reciprocal(qrr[:, p % 2, :], qrr[:, p % 2, :]))
                            gain = ncol[:, 12 + p // 4:13 + p // 4]
                            dve.scalar_tensor_tensor(qn[:, p % 2, :], qr[:, p % 2, :], gain, qrr[:, p % 2, :],
                                                     ALU.mult, ALU.mult).then_inc(s_qn, 1)
                    for what, p in AUX_D[j]:
                        dve.wait_ge(s_ad, ND * g + nd + 1)
                        src = aux_d[nd % 2][:, 0:GT]
                        nd += 1
                        if what == "bonus":
                            dve.wait_ge(o_bon, 64 * g + 16 * p + 16)
                            dve.tensor_tensor(bon[:, :], src, krv[:, p % 2, 2, :], ALU.mult).then_inc(s_ad_free, 1)
                        else:
                            if p == 0:
                                dve.wait_ge(s_cs, 16 * g + 16)
                            dve.wait_ge(s_qo, 8 * g + p + 1)
                            dve.tensor_tensor(m2[:, :], src, cosin[:, 1, :], ALU.mult).then_inc(s_ad_free, 1)
                            link(dve, ch, dve.tensor_tensor(m1[:, :], qn[:, p % 2, :], cosin[:, 0, :], ALU.mult))
                            dve.wait_ge(o_q, 128 * g + 16 * p + 16)
                            dve.tensor_tensor(qo[:, :], m1[:, :], m2[:, :], ALU.add).then_inc(s_qo, 1)
                    for what, p in AUX_A[j]:
                        if what == "w":
                            k, r = krv[:, p % 2, 0, :], krv[:, p % 2, 1, :]
                            dve.wait_ge(s_aa_free, NA * g + ORDER_A.index(("a", p)) + 3)
                            link(dve, ch, dve.tensor_scalar(za[:, :, :], za[:, :, :], 0.5, 0.5, ALU.mult, ALU.add))
                            dve.tensor_scalar(kmod[:, :], za[:, 1, :], cols[:, PC_KA + p:PC_KA + p + 1],
                                              ncol[:, 8 + p:9 + p], ALU.mult, ALU.add)
                            link(dve, ch, dve.tensor_tensor_scan(cz[:, :], reset[:, :], za[:, 0, :], 0.0, ALU.mult, ALU.add))
                            dve.tensor_tensor(za[:, 0, :], cz[:, :], za[:, 0, :], ALU.subtract).then_inc(s_scan, 1)
                            link(dve, ch, dve.tensor_tensor(kmod[:, :], k, kmod[:, :], ALU.mult))
                            dve.scalar_tensor_tensor(rk[:, :], r, cols[:, PC_RK + p:PC_RK + p + 1], kmod[:, :],
                                                     ALU.mult, ALU.mult).then_inc(s_rk, 1)
                ch.end("project, VectorE")

            for t in range(XT):
                invert_rms(0, t)
            for t in range(XT):
                scale_xT(0, 0, t)
            with dve.Fori(0, NG // 2) as i2:
                for half in range(2):
                    group(2 * i2 + half, half)


UNITS = [(i, s) for i in range(NT) for s in range(i // 4 + 1)]
NU = len(UNITS)
SEG = 4 * P


def width(i, s):
    return min(SEG, (i + 1) * P - s * SEG)


LAG = 6
RE = 8


def attention_steps():
    steps = []
    for k in range(NU + LAG + 2):
        if k < NU:
            steps += [("scores", *UNITS[k])]
        tile_ends = 1 <= k <= NU and (k == NU or UNITS[k][1] == 0)
        if tile_ends:
            steps += [("maxima", UNITS[k - 1][0], 0)]
        if k < NU:
            steps += [("soft", *UNITS[k])]
        if tile_ends:
            steps += [("stats", UNITS[k - 1][0], 0)]
        if 0 <= k + 1 - LAG < NU:
            steps += [("scale", *UNITS[k + 1 - LAG])]
        if 0 <= k - LAG < NU:
            steps += [("combine", *UNITS[k - LAG])]
        if 0 <= k - LAG - 1 < NU:
            steps += [("turn", *UNITS[k - LAG - 1])]
        if 0 <= k - LAG - 2 < NU:
            i, s = UNITS[k - LAG - 2]
            steps += [("values", i, s)] + ([("out", i, 0)] if s == i // 4 else [])
    return steps


def attend(nc, io, dr):
    with ExitStack() as ctx:
        m = Pool(nc, ctx, "at")
        qz = m.sb("qz", [P, 2, S])
        kT = m.sb("kT", [P, S])
        vh = m.sb("vh", [P, NT, P])
        ident = m.sb("ident", [P, P])
        mask = m.sb("mask", [P, 2, P])
        lams = m.sb("lams", [P, 4, 64])
        lam = m.sb("lam", [P, 8])
        sign = m.sb("sign", [P, 2])
        e = m.sb("e", [P, RE, 2, SEG])
        pd = m.sb("pd", [P, 4, SEG])
        tt = m.sb("tt", [P, 2, SEG])
        pt = m.sb("pt", [P, 2, SEG])
        osb = m.sb("osb", [P, 2, P])
        nmx = m.sb("nmx", [P, RE, 2, 4])
        sums = m.sb("sums", [P, RE, 2, 4])
        f = m.sb("f", [P, RE, 2, 4])
        cf = m.sb("cf", [P, RE, 2, 4])
        small = m.sb("small", [P, 4, 2])

        sc = [m.ps(f"sc{n}", [P, 2, SEG]) for n in range(2)]
        ptp = [m.ps(f"ptp{n}", [P, SEG]) for n in range(2)]
        op = [m.ps(f"op{n}", [P, 512]) for n in range(2)]

        s_const = m.sem("const")
        s_sign = m.sem("sign_done")
        s_lam = m.sem("lam_chain")
        s_ld = m.sem("ld")
        s_qz = m.sem("qz_zero")
        s_ldv = m.sem("ldv")
        s_sc = m.sem("scores")
        s_mx = m.sem("mx")
        s_exp = m.sem("exp")
        s_df = m.sem("df")
        s_f = m.sem("f_done")
        s_cf = m.sem("cf_done")
        s_t = m.sem("t")
        s_pd = m.sem("pd_done")
        s_tr = m.sem("tr")
        s_pt = m.sem("pt_done")
        s_pv = m.sem("pv")
        s_o = m.sem("o")
        s_dve = m.sem("dve")
        o_o = [m.sem(f"o_o{n}") for n in range(2)]
        block = ctx.enter_context(nc.Block())
        STEPS = attention_steps()

        def unit(i, s):
            return UNITS.index((i, s))

        def units_before(i):
            return UNITS.index((i, 0)) if i >= 0 else UNITS.index((i + NT, 0)) - NU

        @block.sync
        def _(sp):
            for dst, src in ((ident[:, :], io["c_ident"]), (mask[:, :, :], io["c_mask"]), (lams[:, :, :], io["lams"])):
                sp.dma_start(dst, src).then_inc(s_const, 16)
            sp.wait_ge(s_qz, 1)
            with sp.Fori(0, H_A) as h:
                sp.wait_ge(s_sc, NU * h + 1)
                for c in range(2):
                    rows = slice(64 * c, 64 * c + 64)
                    sp.dma_start(qz[rows, c, :], dr["qk"][bass.ds(h, 1), rows, :].rearrange("a p n -> (a p) n"))\
                        .then_inc(s_ld, 16)
                sp.dma_start(kT[:, :], dr["qk"][bass.ds(h + H_A, 1)].rearrange("a p n -> (a p) n")).then_inc(s_ld, 16)
                sp.wait_ge(s_pv, NU * h + NU)
                sp.dma_start(vh[:, :, :], dr["v"][:, bass.ds(h * P, P)].rearrange("(t p) n -> p t n", p=P))\
                    .then_inc(s_ldv, 16)
                for i in range(NT):
                    sp.wait_ge(s_o, NT * h + i + NT + 1)
                    sp.dma_start(dr["o"][i * P:(i + 1) * P, bass.ds(h * P, P)], osb[:, i % 2, :])\
                        .then_inc(o_o[i % 2], 16)
            for n in range(2):
                sp.wait_ge(o_o[n], 16 * NT // 2 * H_A + 16)

        @block.tensor
        def _(pe):
            pe.sem_inc(s_sc, 1)
            pe.sem_inc(s_tr, NU)
            pe.sem_inc(s_pv, NU)
            pe.wait_ge(s_const, 48)
            pe.wait_ge(s_sign, 1)
            with pe.Fori(0, H_A) as h:
                pe.wait_ge(s_ld, 48 * h + 48)
                for kind, i, s in STEPS:
                    if kind == "scores":
                        u, w = unit(i, s), width(i, s)
                        pe.wait_ge(s_exp, NU * h + u + 1)
                        for c in range(2):
                            diag = s == i // 4
                            ins = pe.matmul(sc[u % 2][:, c, 0:w], qz[:, c, i * P:(i + 1) * P],
                                            kT[:, s * SEG:s * SEG + w], start=True, stop=not diag)
                            if diag:
                                ins = pe.matmul(sc[u % 2][:, c, w - P:w], mask[:, 0, :], mask[:, 1, :],
                                                start=False, stop=True)
                        ins.then_inc(s_sc, 1)
                    if kind == "turn":
                        u = unit(i, s)
                        pe.wait_ge(s_pd, NU * h + NU + u + 1)
                        pe.wait_ge(s_pt, NU * h + NU + u - 1)
                        for b in range(width(i, s) // P):
                            ins = pe.transpose(ptp[u % 2][:, b * P:(b + 1) * P],
                                               pd[:, u % 4, b * P:(b + 1) * P], ident[:, :])
                        ins.then_inc(s_tr, 1)
                    if kind == "values":
                        u = unit(i, s)
                        pe.wait_ge(s_pt, NU * h + NU + u + 1)
                        if u == 0:
                            pe.wait_ge(s_ldv, 16 * h + 16)
                        if s == 0:
                            pe.wait_ge(s_o, NT * h + NT + i - 1)
                        for b in range(width(i, s) // P):
                            n = 4 * s + b
                            ins = pe.matmul(op[i % 2][:, 0:P], pt[:, u % 2, b * P:(b + 1) * P], vh[:, n, :],
                                            start=(n == 0), stop=(n == i))
                        ins.then_inc(s_pv, 1)

        @block.scalar
        def _(act):
            act.sem_inc(s_exp, 2)
            act.sem_inc(s_pt, NU)
            act.wait_ge(s_lam, 3)
            act.activation(lam[:, 2:4], lam[:, 0:2], ACT.Exp).then_inc(s_lam, 1)
            with act.Fori(0, H_A) as h:
                for kind, i, s in STEPS:
                    if kind == "soft":
                        u, w = unit(i, s), width(i, s)
                        act.wait_ge(s_mx, NU * h + u + 1)
                        act.wait_ge(s_pd, NU * h + NU + u + 1 - RE)
                        for c in range(2):
                            ins = act.activation(e[:, u % RE, c, 0:w], sc[u % 2][:, c, 0:w], ACT.Exp,
                                                 bias=nmx[:, i % RE, c, s:s + 1], accum_out=sums[:, i % RE, c, s:s + 1])
                        ins.then_inc(s_exp, 1)
                    if kind == "maxima":
                        n = i // 4 + 1
                        act.wait_ge(s_df, NT * h + i + 1)
                        act.activation(f[:, i % RE, :, 0:n], f[:, i % RE, :, 0:n], ACT.Exp).then_inc(s_f, 1)
                    if kind == "scale":
                        u, w = unit(i, s), width(i, s)
                        act.wait_ge(s_cf, NT * h + i + 1)
                        act.wait_ge(s_pd, NU * h + NU + u - 1)
                        act.activation(tt[:, u % 2, 0:w], e[:, u % RE, 1, 0:w], ACT.Copy,
                                       scale=cf[:, i % RE, 1, s:s + 1]).then_inc(s_t, 1)
                    if kind == "turn":
                        u, w = unit(i, s), width(i, s)
                        act.wait_ge(s_tr, NU * h + NU + u + 1)
                        act.wait_ge(s_pv, NU * h + NU + u - 1)
                        act.activation(pt[:, u % 2, 0:w], ptp[u % 2][:, 0:w], ACT.Copy).then_inc(s_pt, 1)

        @block.vector
        def _(dve):
            dve.memset(qz[:, :, :], 0.0).then_inc(s_qz, 1)
            dve.sem_inc(s_pd, NU)
            dve.sem_inc(s_o, NT)
            for n in range(2):
                dve.sem_inc(o_o[n], 16)
            dve.wait_ge(s_const, 48)
            pairs = lams[:, :, :].rearrange("p (a b) n -> p a b n", b=2)
            dve.tensor_tensor(pairs[:, :, 0, :], pairs[:, :, 0, :], pairs[:, :, 1, :], ALU.mult).then_inc(s_lam, 2)
            dve.wait_ge(s_lam, 2)
            dve.tensor_reduce(lam[:, 0:2], pairs[:, :, 0, :], AX, ALU.add).then_inc(s_lam, 1)
            dve.wait_ge(s_lam, 4)
            dve.tensor_tensor(lam[:, 4:5], lam[:, 3:4], lam[:, 2:3], ALU.subtract).then_inc(s_lam, 1)
            dve.memset(sign[:, 0:1], 1.0)
            dve.wait_ge(s_lam, 5)
            dve.tensor_scalar(sign[:, 1:2], lam[:, 4:5], -LAMBDA_INIT, None, ALU.add).then_inc(s_sign, 1)
            dve.wait_ge(s_sign, 1)
            with dve.Fori(0, H_A) as h:
                ch = Count(s_dve, h, 5 * NT)
                for kind, i, s in STEPS:
                    if kind == "soft":
                        u, w = unit(i, s), width(i, s)
                        dve.wait_ge(s_sc, NU * h + u + 2)
                        dve.tensor_reduce(nmx[:, i % RE, :, s], sc[u % 2][:, :, 0:w], AX, ALU.max, negate=True)\
                            .then_inc(s_mx, 1)
                    if kind in ("maxima", "stats"):
                        n, r = i // 4 + 1, i % RE
                        nm, den, rd, rs = (small[:, k, :] for k in range(4))
                    if kind == "maxima":
                        dve.wait_ge(s_mx, NU * h + units_before(i) + n)
                        link(dve, ch, dve.tensor_reduce(nm, nmx[:, r, :, 0:n], AX, ALU.min))
                        dve.tensor_tensor(f[:, r, :, 0:n], wide(nm, n), nmx[:, r, :, 0:n], ALU.subtract).then_inc(s_df, 1)
                    if kind == "stats":
                        dve.wait_ge(s_f, NT * h + i + 1)
                        link(dve, ch, dve.tensor_tensor(cf[:, r, :, 0:n], f[:, r, :, 0:n], sums[:, r, :, 0:n], ALU.mult))
                        link(dve, ch, dve.tensor_reduce(den, cf[:, r, :, 0:n], AX, ALU.add))
                        link(dve, ch, dve.reciprocal(rd, den))
                        link(dve, ch, dve.tensor_tensor(rs, rd, sign[:, :], ALU.mult))
                        dve.tensor_tensor(cf[:, r, :, 0:n], f[:, r, :, 0:n], wide(rs, n), ALU.mult).then_inc(s_cf, 1)
                        dve.wait_ge(s_cf, NT * h + i + 1)
                    if kind == "combine":
                        u, w = unit(i, s), width(i, s)
                        dve.wait_ge(s_t, NU * h + u + 1)
                        dve.wait_ge(s_tr, NU * h + NU + u - 3)
                        dve.scalar_tensor_tensor(pd[:, u % 4, 0:w], e[:, u % RE, 0, 0:w],
                                                 cf[:, i % RE, 0, s:s + 1], tt[:, u % 2, 0:w], ALU.mult, ALU.add)\
                            .then_inc(s_pd, 1)
                    if kind == "out":
                        dve.wait_ge(s_pv, NU * h + NU + units_before(i) + i // 4 + 1)
                        dve.wait_ge(o_o[i % 2], 8 * NT * h + 16 * (i // 2) + 16)
                        dve.tensor_copy(osb[:, i % 2, :], op[i % 2][:, 0:P]).then_inc(s_o, 1)
                ch.end("attend, VectorE")


SERIAL = ("s1", "s2", "s3", "y1", "y2", "y3")
PE_ORDER = ("gl", "gb", "s1", "r1", "s2", "r2", "tok", "r3", "s3", "r4", "y1", "r5", "y2", "r6", "y3", "r7", "gk", "r8")
ACT_ORDER = ("s1", "r1", "s2", "r2", "tok", "r3", "r5", "y3", "r7")
DVE_ORDER = ("gl", "gb", "r2", "r3", "r4", "s3", "r6", "gk", "r8")


class Pieces:

    def __init__(self, sem, order, c, has_pre=True, has_serial=True):
        self.sem = sem
        self.base = sum(n not in SERIAL for n in order) + len(order) * c if has_serial else 0
        self.names = [n for n in order if (has_pre or n in SERIAL) and (has_serial or n not in SERIAL)]

    def before(self):
        return self.base

    def after(self, name):
        return self.base + (self.names.index(name) + 1)


def recur(nc, io, dr):
    with ExitStack() as ctx:
        m = Pool(nc, ctx, "rw")
        raw = m.sb("raw", [P, 2, NPAIR, ROW])
        cin = [m.sb(f"cin{x}", [P, NPAIR, ROW]) for x in range(2)]
        eye = m.sb("eye", [P, C])
        mgb = m.sb("mgb", [P, 2 * C])
        mgk = m.sb("mgk", [P, 2 * C])
        mgl = m.sb("mgl", [P, 3, C])
        gb = [m.sb(f"gb{x}", [P, NPAIR, 2 * C]) for x in range(2)]
        gk = [m.sb(f"gk{x}", [P, NPAIR, 2 * C]) for x in range(2)]
        gl = m.sb("gl", [P, NPAIR, 3, C])
        w = m.sb("w", [P, NPAIR, 3, C])
        lu4 = m.sb("lu4", [P, 2, NPAIR, C])
        l8 = m.sb("l8", [P, NPAIR, C])
        q = [m.sb(f"q{n}", [P, NPAIR, C]) for n in range(4)]
        ty = m.sb("ty", [P, 2, 2, NPAIR, C])
        q5 = [m.sb(f"q5{x}", [P, NPAIR, C]) for x in range(2)]
        tbk = [m.sb(f"tbk{x}", [P, NPAIR, 2, C]) for x in range(2)]
        tv = [m.sb(f"tv{x}", [P, NPAIR, C]) for x in range(2)]
        sa0 = m.sb("sa0", [P, NPAIR, C])
        sa = m.sb("sa", [P, NPAIR, C])
        ds_ = m.sb("ds", [P, NPAIR, C])
        state = m.sb("state", [P, NPAIR, C])
        y = m.sb("y", [P, NPAIR, S])
        zero = m.sb("zero", [P, D])
        ps = [m.ps(f"ps{n}", [P, 512]) for n in range(8)]

        s_const = m.sem("const")
        s_ld = [m.sem(f"ld{x}") for x in range(2)]
        s_cin = m.sem("cin_done")
        s_pe = m.sem("pe")
        s_act = m.sem("act")
        s_dve = m.sem("dve")
        s_init = m.sem("init")
        s_dchain = m.sem("dchain")
        s_masked = m.sem("masked")
        s_out = m.sem("out")
        s_zero, o_zero = m.sem("zero_done"), m.sem("o_zero")
        s_apart, s_apart2 = m.sem("apart"), m.sem("apart2")
        block = ctx.enter_context(nc.Block())
        TURNS = NCH // 2 - 1

        def quarter(n, k=0):
            return ps[n][:, 256 * k:256 * k + 256].rearrange("p (a n) -> p a n", n=C)

        def pairs(n, width=2 * C):
            return ps[n][:, :].rearrange("p (a n) -> p a n", n=width)

        @block.sync
        def _(sp):
            for dst, src in ((eye[:, :], io["c_eye"]), (mgb[:, :], io["c_mgb"]), (mgk[:, :], io["c_mgk"]),
                             (mgl[:, :, :], io["c_mgl"])):
                sp.dma_start(dst, src).then_inc(s_const, 16)
            for x in range(2):
                sp.dma_start(raw[:, x], dr["chunks"][x]).then_inc(s_ld[x], 16)
            assert NB - NE == NCH

            def clear(n):
                sp.dma_start(dr["slots"][bass.ds((NE + n) * P, P), :], zero[:, :]).then_inc(o_zero, 16)

            sp.wait_ge(s_zero, 1)
            for n in range(NCH - 2, NCH):
                clear(n)
            with sp.Fori(0, TURNS) as i:
                for x in range(2):
                    sp.wait_ge(s_cin, 2 * i + x + 1)
                    sp.dma_start(raw[:, x], dr["chunks"][bass.ds(2 * i + x + 2, 1)].rearrange("c p a n -> (c p) a n"))\
                        .then_inc(s_ld[x], 16)
                    clear(2 * i + x)
            sp.wait_ge(s_act, Pieces(s_act, ACT_ORDER, NCH - 1, has_pre=False).after("y3"))
            sp.dma_start(dr["y"].rearrange("a p n -> p a n"), y[:, :, :]).then_inc(s_out, 16)
            sp.wait_ge(s_out, 16)
            sp.wait_ge(o_zero, 16 * NCH)

        @block.gpsimd
        def _(pool):
            pool.memset(zero[:, :], 0.0).then_inc(s_zero, 1)
            for x in range(2):
                pool.wait_ge(s_ld[x], 16)
                pool.tensor_copy(cin[x][:, :, :], raw[:, x]).then_inc(s_cin, 1)
            with pool.Fori(0, TURNS) as i:
                for x in range(2):
                    pool.wait_ge(s_ld[x], 16 * i + 32)
                    pool.wait_ge(s_pe, Pieces(s_pe, PE_ORDER, 2 * i + x).after("y1"))
                    pool.wait_ge(s_dve, Pieces(s_dve, DVE_ORDER, 2 * i + x).after("s3"))
                    pool.sem_inc(s_apart2, 1)
                    pool.tensor_copy(cin[x][:, :, :], raw[:, x]).then_inc(s_cin, 1)

        HALVES = [slice(0, C), slice(C, P)]

        @block.tensor
        def _(pe):
            def half(c, x, has_pre=True, has_serial=True):
                a = Pieces(s_act, ACT_ORDER, c, has_pre, has_serial)
                d = Pieces(s_dve, DVE_ORDER, c, has_pre, has_serial)
                nx = 1 - x if has_serial else x

                def product(out, lhs, rhs, start=True, stop=True):
                    return pe.matmul(out, lhs, rhs, start=start, stop=stop)

                def every(*products, parted=True):
                    if parted:
                        pe.sem_inc(s_apart, 1)
                    for p in range(NPAIR):
                        for f in products:
                            for rows in HALVES:
                                ins = f(p, rows)
                    ins.then_inc(s_pe, 1)

                A, R, B, K, V = (slice(n * C, (n + 1) * C) for n in range(5))
                AR = slice(0, 2 * C)
                U = slice(0, C)
                if has_pre:
                    pe.wait_ge(s_cin, c + 2 if has_serial else 1)
                    every(lambda p, r: product(quarter(1)[r, p, :], cin[nx][r, p, A], cin[nx][r, p, B]))
                    every(lambda p, r: product(pairs(0)[r, p, :], cin[nx][r, p, B], cin[nx][r, p, AR]), parted=False)
                if has_serial:
                    pe.wait_ge(s_dve, d.before())
                    pe.wait_ge(s_act, a.before())
                    every(lambda p, r: product(quarter(2)[r, p, :], cin[x][r, p, A], state[r, p, :], stop=False),
                          lambda p, r: product(quarter(2)[r, p, :], gk[x][r, p, 0:C], tv[x][r, p, :], start=False))
                if has_pre:
                    pe.wait_ge(s_dve, d.after("gb"))
                    every(lambda p, r: product(pairs(3)[r, p, 0:C], gl[r, p, 0, :], gb[nx][r, p, U]),
                          lambda p, r: product(pairs(3)[r, p, C:2 * C], gb[nx][r, p, U], gl[r, p, 0, :]))
                if has_serial:
                    pe.wait_ge(s_act, a.after("s1"))
                    every(lambda p, r: product(quarter(4)[r, p, :], q5[x][r, p, :], sa0[r, p, :]))
                if has_pre:
                    pe.wait_ge(s_act, a.after("r1"))
                    every(lambda p, r: product(pairs(5)[r, p, :], w[r, p, 2, :], w[r, p, 0:2, :].rearrange("p a n -> p (a n)")),
                          lambda p, r: product(quarter(6)[r, p, :], w[r, p, 1, :], w[r, p, 2, :]))
                    every(lambda p, r: product(pairs(7)[r, p, 0:C], cin[nx][r, p, B], eye[r, :]),
                          lambda p, r: product(pairs(7)[r, p, C:2 * C], cin[nx][r, p, K], eye[r, :]),
                          lambda p, r: product(quarter(1)[r, p, :], cin[nx][r, p, V], eye[r, :]), parted=False)
                    pe.wait_ge(s_act, a.after("r2"))
                    pe.wait_ge(s_dve, d.after("r2"))
                    every(lambda p, r: product(quarter(0)[r, p, :], lu4[r, 0, p, :], q[0][r, p, :]),
                          lambda p, r: product(quarter(2)[r, p, :], lu4[r, 1, p, :], lu4[r, 0, p, :]))
                if has_serial:
                    pe.wait_ge(s_act, a.after("s2"))
                    every(lambda p, r: product(quarter(3)[r, p, :], tbk[x][r, p, 0, :], sa[r, p, :], stop=False),
                          lambda p, r: product(quarter(3)[r, p, :], tbk[x][r, p, 1, :], tv[x][r, p, :], start=False))
                if has_pre:
                    pe.wait_ge(s_act, a.after("r3"))
                    pe.wait_ge(s_dve, d.after("r3"))
                    every(lambda p, r: product(quarter(4)[r, p, :], l8[r, p, :], q[1][r, p, :]))
                if has_serial:
                    every(lambda p, r: product(quarter(5)[r, p, :], state[r, p, :], cin[x][r, p, R], p == 0, False), parted=False)
                if has_pre:
                    pe.wait_ge(s_dve, d.after("r4"))
                    every(lambda p, r: product(quarter(6, 0)[r, p, :], q[2][r, p, :], eye[r, :]),
                          lambda p, r: product(quarter(6, 1)[r, p, :], gl[r, p, 1, :], q[2][r, p, :]))
                if has_serial:
                    every(lambda p, r: product(quarter(5)[r, p, :], tv[x][r, p, :], gk[x][r, p, C:2 * C], False, False),
                          parted=False)
                if has_pre:
                    pe.wait_ge(s_act, a.after("r5"))
                    every(lambda p, r: product(quarter(0)[r, p, :], ty[r, 0, 0, p, :], ty[r, 0, 1, p, :]))
                if has_serial:
                    every(lambda p, r: product(quarter(5)[r, p, :], sa[r, p, :], gb[x][r, p, C:2 * C], False, p == NPAIR - 1),
                          parted=False)
                if has_pre:
                    pe.wait_ge(s_dve, d.after("r6"))
                    every(lambda p, r: product(quarter(7, 0)[r, p, :], q[3][r, p, :], eye[r, :]),
                          lambda p, r: product(quarter(7, 1)[r, p, :], gl[r, p, 2, :], q[3][r, p, :]))
                    every(lambda p, r: product(pairs(2)[r, p, :], cin[nx][r, p, K], cin[nx][r, p, AR]), parted=False)
                    pe.wait_ge(s_act, a.after("r7"))
                    every(lambda p, r: product(quarter(4)[r, p, :], ty[r, 1, 0, p, :], ty[r, 1, 1, p, :]))

            pe.wait_ge(s_const, 64)
            pe.wait_ge(s_init, 1)
            half(0, 0, has_serial=False)
            with pe.Fori(0, TURNS) as i:
                for x in range(2):
                    half(2 * i + x, x)
            half(NCH - 2, 0)
            half(NCH - 1, 1, has_pre=False)

        @block.scalar
        def _(act):
            def half(c, x, has_pre=True, has_serial=True):
                t = Pieces(s_pe, PE_ORDER, c, has_pre, has_serial)
                nx = 1 - x if has_serial else x

                def piece(name, *copies):
                    act.wait_ge(s_pe, t.after(name))
                    for dst, src in copies:
                        ins = act.activation(dst, src, ACT.Copy)
                    ins.then_inc(s_act, 1)

                if has_serial:
                    piece("s1", (sa0[:, :, :], quarter(2)))
                if has_pre:
                    piece("r1", (w[:, :, 1:3, :].rearrange("p a b n -> p a (b n)"), pairs(3)))
                if has_serial:
                    piece("s2", (sa[:, :, :], quarter(4)))
                if has_pre:
                    piece("r2", (lu4[:, 0], quarter(6)))
                    piece("tok", (tbk[nx][:, :, :, :].rearrange("p a b n -> p a (b n)"), pairs(7)), (tv[nx][:, :, :], quarter(1)))
                    piece("r3", (l8[:, :, :], quarter(2)))
                    piece("r5", (ty[:, 0].rearrange("p a b n -> p (a b n)"), ps[6][:, :]))
                if has_serial:
                    piece("y3", (y[:, :, bass.ds(c * C, C)], quarter(5)))
                if has_pre:
                    piece("r7", (ty[:, 1].rearrange("p a b n -> p (a b n)"), ps[7][:, :]))

            half(0, 0, has_serial=False)
            with act.Fori(0, TURNS) as i:
                for x in range(2):
                    half(2 * i + x, x)
            half(NCH - 2, 0)
            half(NCH - 1, 1, has_pre=False)

        @block.vector
        def _(dve):
            def half(c, x, has_pre=True, has_serial=True):
                t = Pieces(s_pe, PE_ORDER, c, has_pre, has_serial)
                d = Pieces(s_dve, DVE_ORDER, c, has_pre, has_serial)
                nx = 1 - x if has_serial else x
                def add(name, bank, old, new):
                    dve.wait_ge(s_pe, t.after(name))
                    if name == "r2":
                        dve.tensor_copy(lu4[:, 1], pairs(bank)[:, :, C:2 * C])
                        src = pairs(bank)[:, :, 0:C]
                    else:
                        src = quarter(bank)
                    dve.tensor_tensor(new[:, :, :], src, old, ALU.add).then_inc(s_dve, 1)

                if has_pre:
                    dve.wait_ge(s_pe, t.after("gl"))
                    dve.tensor_tensor(gl[:, :, :, :], quarter(1).unsqueeze(2).broadcast_to([P, NPAIR, 3, C]),
                                      mgl[:, :, :].unsqueeze(1).broadcast_to([P, NPAIR, 3, C]), ALU.mult).then_inc(s_dve, 1)
                    dve.wait_ge(s_pe, t.after("gb"))
                    dve.tensor_tensor(gb[nx][:, :, :], pairs(0), middle(mgb[:, :], NPAIR), ALU.mult).then_inc(s_masked, 1)
                    dve.wait_ge(s_masked, c + 2 if has_serial else 1)
                    dve.tensor_tensor(w[:, :, 0, :], gb[nx][:, :, 0:C], middle(eye[:, :], NPAIR), ALU.add).then_inc(s_dve, 1)
                    add("r2", 5, w[:, :, 0, :], q[0])
                    add("r3", 0, q[0][:, :, :], q[1])
                    add("r4", 4, q[1][:, :, :], q[2])
                if has_serial:
                    dve.wait_ge(s_pe, t.after("y1"))
                    dve.tensor_tensor(ds_[:, :, :], quarter(3), state[:, :, :], ALU.add).then_inc(s_dchain, 1)
                    dve.wait_ge(s_dchain, c + 1)
                    dve.tensor_tensor(state[:, :, :], ds_[:, :, :], cin[x][:, :, 5 * C:5 * C + 1].broadcast_to([P, NPAIR, C]),
                                      ALU.mult).then_inc(s_dve, 1)
                if has_pre:
                    add("r6", 0, q[2][:, :, :], q[3])
                    dve.wait_ge(s_pe, t.after("gk"))
                    dve.tensor_tensor(gk[nx][:, :, :], pairs(2), middle(mgk[:, :], NPAIR), ALU.mult).then_inc(s_dve, 1)
                    add("r8", 4, q[3][:, :, :], q5[nx])

            dve.memset(state[:, :, :], 0.0).then_inc(s_init, 1)
            dve.wait_ge(s_const, 64)
            half(0, 0, has_serial=False)
            with dve.Fori(0, TURNS) as i:
                for x in range(2):
                    half(2 * i + x, x)
            half(NCH - 2, 0)
            half(NCH - 1, 1, has_pre=False)


NEG = -1e30


def merge(nc, io, dr, keep):
    with ExitStack() as ctx:
        m = Pool(nc, ctx, "mg")
        w_out = m.sb("w_out", [P, KC, D])
        w_rt = m.sb("w_rt", [P, KC, 4 + NE])
        b_rt = m.sb("b_rt", [P, 4 + NE])
        cols = m.sb("cols", [P, PC_N])
        subln = m.sb("subln", [P, P])
        ident = m.sb("ident", [P, P])
        mean2 = m.sb("mean2", [P, P])
        giota = m.sb("giota", [P, NE])
        eiota = m.sb("eiota", [P, NE])
        eps = m.sb("eps", [P, 3])
        yin = m.sb("yin", [P, 2, 3, NPAIR, GT])
        oin = m.sb("oin", [P, 2, XT, DA])
        xin = m.sb("xin", [P, 2, XT, D])
        sq = m.sb("sq", [P, D])
        osq = m.sb("osq", [P, DA])
        rinv = m.sb("rinv", [P, D])
        ost = m.sb("ost", [P, XT, 2, H_A])
        mix = m.sb("mix", [P, 2, 2 * NPAIR, GT])
        hb = m.sb("hb", [P, XT, D])
        hsq = m.sb("hsq", [P, D])
        hn = m.sb("hn", [P, XT, D])
        st = m.sb("st", [P, 3, XT])
        tT = m.sb("tT", [P, KC, P])
        lg = m.sb("lg", [P, 4 + NE])
        g8 = m.sb("g8", [P, 8])
        m8 = m.sb("m8", [P, 8])
        i8 = m.sb("i8", [P, 8], U32)
        gi = m.sb("gi", [P, 1])
        eg = m.sb("eg", [P, 4])
        pen = m.sb("pen", [P, NE])
        v8 = m.sb("v8", [P, 8])
        j8 = m.sb("j8", [P, 8], U32)
        ji = m.sb("ji", [P, 2])
        sm = m.sb("sm", [P, 8])

        pm = m.ps("pm", [P, 2, 512])
        pt = m.ps("pt", [P, 512])
        pr = m.ps("pr", [P, 512])
        po = m.ps("po", [P, 2, 512])
        ph = m.ps("ph", [P, KC, P])

        s_const, s_init, s_wout = m.sem("const"), m.sem("init"), m.sem("wout")
        s_y = [m.sem(f"y_ld{x}") for x in range(2)]
        s_o = [m.sem(f"o_ld{x}") for x in range(2)]
        s_x = [m.sem(f"x_ld{x}") for x in range(2)]
        s_mean, s_var = m.sem("mean"), m.sem("var")
        s_oT, s_proj, s_hT, s_route = m.sem("oT"), m.sem("proj"), m.sem("hT"), m.sem("route")
        s_sq, s_sd = m.sem("sq"), m.sem("sd")
        s_osd, s_oTc, s_hsq, s_hsd = m.sem("osd"), m.sem("oTc"), m.sem("hsq"), m.sem("hsd")
        s_hn, s_eg, s_e2 = m.sem("hn"), m.sem("eg"), m.sem("e2")
        s_d, s_mix = m.sem("d"), m.sem("mix")
        s_osq, s_on, s_rstd, s_tT = m.sem("osq"), m.sem("on"), m.sem("rstd"), m.sem("tT")
        s_v8 = m.sem("v8")
        s_h = m.sem("h")
        s_gmax = m.sem("gmax")
        s_ch = m.sem("chain")
        s_apart = m.sem("apart")
        o_h = [m.sem(f"o_h{t}") for t in range(XT)]
        o_hn = [m.sem(f"o_hn{t}") for t in range(XT)]
        block = ctx.enter_context(nc.Block())
        consts = [(w_rt[:, :, :], io["w_rt"]),
                  (b_rt[:, :], io["b_rt"]), (cols[:, :], io["cols"]), (subln[:, :], io["subln"]),
                  (ident[:, :], io["c_ident"]), (mean2[:, :], io["c_mean2"]), (giota[:, :], io["c_giota"]),
                  (eiota[:, :], io["c_eiota"])]
        N_CONST = 16 * len(consts)

        def turns(eng, turn):
            def peeled(T):
                turn(T // 2, T % 2, -1 <= T <= NG - 2, T <= NG - 3, 0 <= T < NG, T > 0)

            for T in range(-2, 2):
                peeled(T)
            with eng.Fori(1, NG // 2 - 1) as i:
                for x in range(2):
                    turn(i, x, True, True, True, True)
            for T in range(NG - 2, NG + 1):
                peeled(T)

        def half(i, x, ahead):
            return i + (x + ahead) // 2, (x + ahead) % 2

        @block.sync
        def _(sp):
            def load_yo(i, x):
                cols_g = bass.ds((2 * i + x) * GT, GT)
                for n, src in enumerate((dr["y"], dr["bonus"], dr["g"])):
                    sp.dma_start(yin[:, x, n], src[:, :, cols_g].rearrange("a p n -> p a n")).then_inc(s_y[x], 16)
                sp.dma_start(oin[:, x], dr["o"][cols_g, :].rearrange("(t p) n -> p t n", p=P)).then_inc(s_o[x], 16)

            def load_x(i, x):
                cols_g = bass.ds((2 * i + x) * GT, GT)
                sp.dma_start(xin[:, x], io["x"][cols_g, :].rearrange("(t p) n -> p t n", p=P)).then_inc(s_x[x], 16)

            def turn(i, x, prep, mean, main, late):
                T = 2 * i + x
                if not main:
                    return
                if mean:
                    sp.wait_ge(s_mix, T + 1)
                    sp.wait_ge(s_oT, 2 * T + 2)
                    load_yo(i + 1, x)
                for t in range(XT):
                    rows = bass.ds(T * GT + t * P, P)
                    sp.wait_ge(s_h, 2 * T + t + 2)
                    sp.dma_start(dr["h"][rows, :], hb[:, t, :]).then_inc(o_h[t], 16)
                    if mean and t == XT - 1:
                        load_x(i + 1, x)
                    sp.wait_ge(s_hn, 2 * T + t + 1)
                    sp.dma_start(dr["hn"][rows, :], hn[:, t, :]).then_inc(o_hn[t], 16)

            load_yo(0, 0)
            for dst, src in consts:
                sp.dma_start(dst, src).then_inc(s_const, 16)
            load_yo(0, 1)
            sp.dma_start(w_out[:, :, :], io["w_out"][0].rearrange("(k p) n -> p k n", p=P)).then_inc(s_wout, 16)
            load_x(0, 0)
            load_x(0, 1)
            turns(sp, turn)
            for t in range(XT):
                sp.wait_ge(o_h[t], 16 * NG + 16)
                sp.wait_ge(o_hn[t], 16 * NG + 16)

        @block.tensor
        def _(pe):
            def project_tile(i, x, t):
                T = 2 * i + x
                tok = slice(t * P, (t + 1) * P)
                if isinstance(i, int) and T == 0:
                    pe.wait_ge(s_wout, 16)
                pe.wait_ge(s_oTc, 2 * T + t + 1)
                pe.wait_ge(s_h, 2 * T + t + 1)
                for n in range(2):
                    for k in range(KC):
                        if n == 0 and k == H_A:
                            pe.wait_ge(s_mix, T + 1)
                        ins = pe.matmul(po[:, n, :], mix[:, x, k, tok], w_out[:, k, 512 * n:512 * n + 512],
                                        start=(k == 0), stop=(k == KC - 1))
                ins.then_inc(s_proj, 1)

            def transpose_h(tile, t):
                pe.wait_ge(s_hn, tile + 1)
                for k in range(KC):
                    ins = pe.transpose(ph[:, k, :], hn[:, t, k * P:(k + 1) * P], ident[:, :])
                ins.then_inc(s_hT, 1)

            def route(tile):
                pe.wait_ge(s_tT, tile + 1)
                pe.wait_ge(s_gmax, tile + 1)
                for k in range(KC):
                    ins = pe.matmul(pr[:, 0:4 + NE], tT[:, k, :], w_rt[:, k, :], start=(k == 0), stop=(k == KC - 1))
                ins.then_inc(s_route, 1)

            def transpose_o(i, x, t, first):
                n, z = half(i, x, 1)
                tile = 2 * (2 * n + z) + t
                pe.wait_ge(s_on, tile + 1)
                if not (first and t == 0):
                    pe.wait_ge(s_oTc, tile)
                for h in range(H_A):
                    ins = pe.transpose(pt[:, h * P:(h + 1) * P], oin[:, z, t, h * P:(h + 1) * P], ident[:, :])
                ins.then_inc(s_oT, 1)

            def averages(out_sem, src):
                for n in range(2):
                    ins = pe.matmul(pm[:, n, :], mean2[:, :], src[:, 512 * n:512 * n + 512], start=True, stop=True)
                ins.then_inc(out_sem, 1)

            def turn(i, x, prep, mean, main, late):
                T = 2 * i + x
                if main:
                    project_tile(i, x, 0)
                if late:
                    transpose_h(2 * T - 1, 1)
                if prep:
                    pe.wait_ge(s_sq, T + 2)
                    averages(s_var, sq[:, :])
                if late:
                    route(2 * T - 1)
                if main:
                    project_tile(i, x, 1)
                    transpose_h(2 * T, 0)
                if prep:
                    transpose_o(i, x, 0, not main)
                if mean:
                    n, z = half(i, x, 2)
                    pe.wait_ge(s_y[z], 48 * n + 48)
                    if main or prep:
                        pe.wait_ge(s_sd, T + 2)
                    averages(s_mean, yin[:, z, 0].rearrange("p a n -> p (a n)"))
                if main:
                    route(2 * T)
                if prep:
                    transpose_o(i, x, 1, False)

            pe.wait_ge(s_const, N_CONST)
            turns(pe, turn)

        @block.scalar
        def _(act):
            def square_h(tile, t):
                act.wait_ge(s_h, tile + 2)
                act.activation(hsq[:, :], hb[:, t, :], ACT.Square, accum_out=st[:, 0, t:t + 1]).then_inc(s_hsq, 1)
                act.wait_ge(s_hsq, tile + 1)
                act.activation(st[:, 1, t:t + 1], st[:, 0, t:t + 1], ACT.Sqrt, bias=eps[:, 2:3],
                               scale=1.0 / D).then_inc(s_hsd, 1)

            def norm_h(i, x, t):
                T = 2 * i + x
                act.wait_ge(s_rstd, 2 * T + t + 1)
                act.wait_ge(o_hn[t], 16 * T + 16)
                act.activation(hn[:, t, :], hb[:, t, :], ACT.Copy, scale=st[:, 2, t:t + 1]).then_inc(s_hn, 1)

            def shares(tile):
                act.wait_ge(s_gmax, tile + 2)
                act.activation(eg[:, :], lg[:, 0:4], ACT.Exp, bias=sm[:, 0:1], accum_out=sm[:, 1:2]).then_inc(s_eg, 1)
                act.wait_ge(s_v8, tile + 1)
                act.activation(sm[:, 3:4], v8[:, 1:2], ACT.Exp, bias=sm[:, 2:3]).then_inc(s_e2, 1)

            def turn(i, x, prep, mean, main, late):
                T = 2 * i + x
                n, z = half(i, x, 1)
                if prep:
                    act.wait_ge(s_d, T + 2)
                    if main:
                        act.wait_ge(s_var, T + 1)
                    act.activation(sq[:, :], yin[:, z, 0].rearrange("p a n -> p (a n)"), ACT.Square).then_inc(s_sq, 1)
                    for t in range(XT):
                        act.wait_ge(s_osq, 2 * T + 3 + t)
                        act.activation(ost[:, t, 1, :], ost[:, t, 0, :], ACT.Sqrt, bias=eps[:, 1:2], scale=1.0 / P)\
                            .then_inc(s_osd, 1)
                if late:
                    shares(2 * T - 2)
                if main:
                    square_h(2 * T, 0)
                if prep:
                    act.wait_ge(s_var, T + 2)
                    act.activation(rinv[:, :], pm[:, :, :].rearrange("p a n -> p (a n)"), ACT.Sqrt, bias=eps[:, 0:1])\
                        .then_inc(s_sd, 1)
                if main:
                    norm_h(i, x, 0)
                if late:
                    shares(2 * T - 1)
                if main:
                    square_h(2 * T + 1, 1)
                if prep:
                    for t in range(XT):
                        act.wait_ge(s_oT, 2 * T + 3 + t)
                        act.activation(mix[:, z, 0:H_A, t * P:(t + 1) * P], pt[:, :].rearrange("p (a n) -> p a n", n=P),
                                       ACT.Copy).then_inc(s_oTc, 1)
                if main:
                    norm_h(i, x, 1)

            act.wait_ge(s_const, N_CONST)
            act.wait_ge(s_init, 1)
            turns(act, turn)

        @block.vector
        def _(dve):
            chain = {"base": 0, "n": 0}

            def link(ins):
                chain["n"] += 1
                ins.then_inc(s_ch, 1)
                dve.wait_ge(s_ch, chain["base"] + chain["n"])

            def add_x(i, x, t):
                T = 2 * i + x
                dve.wait_ge(s_proj, 2 * T + t + 1)
                if t == 0:
                    dve.wait_ge(s_x[x], 16 * i + 16)
                dve.wait_ge(o_h[t], 16 * T + 16)
                dve.tensor_tensor(hb[:, t, :], po[:, :, :].rearrange("p a n -> p (a n)"), xin[:, x, t, :], ALU.add)\
                    .then_inc(s_h, 1)

            def invert_sd(tile, t):
                dve.wait_ge(s_hsd, tile + 1)
                dve.reciprocal(st[:, 2, t:t + 1], st[:, 1, t:t + 1]).then_inc(s_rstd, 1)

            def scale_hT(tile):
                dve.wait_ge(s_hT, tile + 1)
                dve.tensor_tensor(tT[:, :, :], ph[:, :, :], wide(cols[:, PC_LN2:PC_LN2 + KC], P), ALU.mult)\
                    .then_inc(s_tT, 1)

            def choose(tile):
                dve.wait_ge(s_route, tile + 1)
                link(dve.tensor_tensor(lg[:, :], pr[:, 0:4 + NE], b_rt[:, :], ALU.add))
                dve.tensor_reduce(sm[:, 0:1], lg[:, 0:4], AX, ALU.max, negate=True).then_inc(s_gmax, 1)
                link(dve.tensor_copy(g8[:, 0:4], lg[:, 0:4]))
                dve.sem_inc(s_apart, 1)
                link(dve.max(m8[:, :], g8[:, :]))
                dve.sem_inc(s_apart, 1)
                link(dve.max_index(i8[:, :], m8[:, :], g8[:, :]))
                link(dve.tensor_copy(gi[:, :], i8[:, 0:1]))
                link(dve.tensor_scalar(pen[:, :], giota[:, :], gi[:, :], NEG, ALU.not_equal, ALU.mult))
                link(dve.tensor_tensor(pen[:, :], pen[:, :], lg[:, 4:], ALU.add))
                dve.sem_inc(s_apart, 1)
                link(dve.max(v8[:, :], pen[:, :]))
                dve.tensor_scalar(sm[:, 2:3], v8[:, 0:1], -1.0, None, ALU.mult).then_inc(s_v8, 1)
                dve.sem_inc(s_apart, 1)
                link(dve.max_index(j8[:, :], v8[:, :], pen[:, :]))
                link(dve.tensor_copy(ji[:, :], j8[:, 0:2]))
                at = bass.ds(tile, 1)
                for n in range(2):
                    dve.tensor_scalar(keep["hot"][:, at, n, :].rearrange("p a n -> p (a n)"), eiota[:, :],
                                      ji[:, n:n + 1], None, ALU.is_equal)
                dve.wait_ge(s_e2, tile + 1)
                link(dve.tensor_scalar(sm[:, 4:5], sm[:, 3:4], 1.0, None, ALU.add))
                link(dve.tensor_tensor(sm[:, 5:6], sm[:, 4:5], sm[:, 1:2], ALU.mult))
                link(dve.reciprocal(sm[:, 6:7], sm[:, 5:6]))
                link(dve.tensor_tensor(sm[:, 7:8], sm[:, 6:7], sm[:, 3:4], ALU.mult))
                link(dve.tensor_copy(keep["gate"][:, at, :].rearrange("p a n -> p (a n)"), sm[:, 6:8]))

            def turn(i, x, prep, mean, main, late):
                T = 2 * i + x
                if not isinstance(i, int) and x == 0:
                    assert chain["n"] == AHEAD, chain
                    chain["base"], chain["n"] = AHEAD + (i - 1) * PER_LOOP, 0
                n, z = half(i, x, 1)
                yf = yin[:, z, 0].rearrange("p a n -> p (a n)")
                o = [oin[:, z, t, :] for t in range(XT)]
                if prep:
                    dve.wait_ge(s_mean, T + 2)
                    dve.wait_ge(s_y[z], 48 * n + 48)
                    dve.tensor_tensor(yf, yf, pm[:, :, :].rearrange("p a n -> p (a n)"), ALU.subtract).then_inc(s_d, 1)
                    dve.wait_ge(s_o[z], 16 * n + 16)
                    for t in range(XT):
                        link(dve.tensor_tensor(osq[:, :], o[t], o[t], ALU.mult))
                        dve.tensor_reduce(ost[:, t, 0, :], osq[:, :].rearrange("p (h n) -> p h n", n=P), AX, ALU.add)\
                            .then_inc(s_osq, 1)
                        dve.wait_ge(s_osq, 2 * T + 3 + t)
                    for t in range(XT):
                        o3 = o[t].rearrange("p (h n) -> p h n", n=P)
                        dve.wait_ge(s_osd, 2 * T + 3 + t)
                        link(dve.reciprocal(ost[:, t, 1, :], ost[:, t, 1, :]))
                        link(dve.tensor_tensor(o3, o3, wide(ost[:, t, 1, :], P), ALU.mult))
                        dve.scalar_tensor_tensor(o3, o3, 1.0 - LAMBDA_INIT, middle(subln[:, :], H_A), ALU.mult, ALU.mult)\
                            .then_inc(s_on, 1)
                if late:
                    choose(2 * T - 2)
                if main:
                    add_x(i, x, 0)
                if late:
                    scale_hT(2 * T - 1)
                if main:
                    invert_sd(2 * T, 0)
                if prep:
                    dve.wait_ge(s_sd, T + 2)
                    link(dve.reciprocal(rinv[:, :], rinv[:, :]))
                    link(dve.tensor_tensor(yf, yf, rinv[:, :], ALU.mult))
                if late:
                    choose(2 * T - 1)
                if main:
                    add_x(i, x, 1)
                    scale_hT(2 * T)
                if prep:
                    for p in range(NPAIR):
                        ins = dve.tensor_scalar(yin[:, z, 0, p], yin[:, z, 0, p], cols[:, PC_LXG + p:PC_LXG + p + 1],
                                                cols[:, PC_LXB + p:PC_LXB + p + 1], ALU.mult, ALU.add)
                    link(ins)
                    link(dve.tensor_tensor(yin[:, z, 0], yin[:, z, 0], yin[:, z, 1], ALU.add))
                    dve.tensor_tensor(mix[:, z, NPAIR:, :], yin[:, z, 0], yin[:, z, 2], ALU.mult).then_inc(s_mix, 1)
                if main:
                    invert_sd(2 * T + 1, 1)
                if not isinstance(i, int) and x == 1:
                    assert chain["n"] == PER_LOOP, chain
                    chain["base"], chain["n"] = AHEAD + (NG // 2 - 2) * PER_LOOP, 0

            PREP_LINKS, CHOOSE_LINKS = 3 * XT + 4, 15
            PER_LOOP = 2 * (PREP_LINKS + 2 * CHOOSE_LINKS)
            AHEAD = 3 * PREP_LINKS + 2 * CHOOSE_LINKS
            for t in range(XT):
                dve.sem_inc(o_h[t], 16)
                dve.sem_inc(o_hn[t], 16)
            dve.sem_inc(s_h, 1)
            dve.sem_inc(s_gmax, 1)
            dve.memset(eps[:, 0:1], 64e-5)
            dve.memset(eps[:, 1:2], 1e-5)
            dve.memset(eps[:, 2:3], 1e-6)
            dve.memset(g8[:, :], NEG)
            dve.memset(lg[:, 0:1], 0.0).then_inc(s_init, 1)
            dve.wait_ge(s_const, N_CONST)
            turns(dve, turn)


def dispatch(nc, io, dr, keep, ahead):
    with ExitStack() as ctx:
        m = Pool(nc, ctx, "ds")
        before = m.sb("before", [P, P])
        ones = m.sb("ones", [P, P])
        blocks = m.sb("blocks", [P, NT])
        picked = m.sb("picked", [P, NT, NE])
        dest = m.sb("dest", [P, NT, NE])
        total = m.sb("total", [P, NT, NE])
        base = m.sb("base", [P, NE])
        more = m.sb("more", [P, NE, NT])
        nb = m.sb("nb", [P, NE])
        ones_e = m.sb("ones_e", [P, NE])
        ends = m.sb("ends", [P, NE])
        nbi = m.sb("nbi", [P, 2, NE], I32)
        tmp = m.sb("tmp", [P, NT, NE])
        slotf = m.sb("slotf", [P, NT, 2])
        ids = m.sb("ids", [P, NT], I32)
        zero = m.sb("zero", [P, NB], I32)
        pr = m.ps("pr", [P, 512])
        pc = m.ps("pc", [P, 512])
        s_const = m.sem("const")
        s_ids = m.sem("ids_done")
        s_zero = m.sem("zero_done")
        s_picked = m.sem("picked_done")
        s_pe = m.sem("pe")
        s_ch = m.sem("chain")
        s_slots = m.sem("slots")
        o_sc = m.sem("o_sc")
        block = ctx.enter_context(nc.Block())

        @block.sync
        def _(sp):
            for dst, src in ((before[:, :], io["c_before"]), (ones[:, :], io["c_ones"]), (blocks[:, :], io["c_blocks"])):
                sp.dma_start(dst, src).then_inc(s_const, 16)
            sp.wait_ge(s_zero, 1)
            sp.dma_start(dr["slot_tok"].rearrange("(p n) a -> p (n a)", p=P), zero[:, :]).then_inc(s_zero, 16)
            ahead(sp)

        @block.gpsimd
        def _(pool):
            pool.memset(zero[:, :], 0).then_inc(s_zero, 1)
            pool.iota(ids[:, :], [[P, NT]], base=0, channel_multiplier=1).then_inc(s_ids, 1)
            pool.wait_ge(s_zero, 17)
            pool.wait_ge(s_slots, 1)
            pool.wait_ge(s_ids, 1)
            for t in range(NT):
                for n in range(2):
                    pool.indirect_dma_start(dr["slot_tok"], bass.IndirectOffsetOnAxis(keep["slot"][:, t, n:n + 1], 0),
                                            ids[:, t:t + 1], None).then_inc(o_sc, 16)
            pool.wait_ge(o_sc, 16 * 2 * NT)

        @block.tensor
        def _(pe):
            pe.wait_ge(s_const, 48)
            pe.wait_ge(s_picked, 1)
            flat = picked[:, :, :].rearrange("p a n -> p (a n)")
            pe.matmul(pr[:, :], before[:, :], flat, start=True, stop=True)
            pe.matmul(pc[:, :], ones[:, :], flat, start=True, stop=True).then_inc(s_pe, 1)

        @block.vector
        def _(dve):
            dve.tensor_tensor(picked[:, :, :], keep["hot"][:, :, 0, :], keep["hot"][:, :, 1, :], ALU.add).then_inc(s_picked, 1)
            n = [0]

            def chain(ins):
                n[0] += 1
                ins.then_inc(s_ch, 1)
                dve.wait_ge(s_ch, n[0])

            dve.wait_ge(s_const, 48)
            dve.wait_ge(s_pe, 1)
            chain(dve.tensor_copy(total[:, :, :].rearrange("p a n -> p (a n)"), pc[:, :]))
            dve.memset(ones_e[:, :], 1.0)
            chain(dve.memset(base[:, :], 0.0))
            for t in range(NT):
                dve.tensor_tensor(dest[:, t, :], pr[:, t * NE:(t + 1) * NE], base[:, :], ALU.add)
                chain(dve.tensor_tensor(base[:, :], base[:, :], total[:, t, :], ALU.add))
            chain(dve.tensor_tensor(more[:, :, :], wide(base[:, :], NT), middle(blocks[:, :], NE), ALU.is_gt))
            chain(dve.tensor_reduce(nb[:, :], more[:, :, :], AX, ALU.add))
            chain(dve.tensor_scalar(nb[:, :], nb[:, :], 1.0, None, ALU.add))
            chain(dve.tensor_tensor_scan(ends[:, :], ones_e[:, :], nb[:, :], 0.0, ALU.mult, ALU.add))
            dve.tensor_copy(nbi[:, 1, :], nb[:, :])
            chain(dve.tensor_tensor(ends[:, :], ends[:, :], nb[:, :], ALU.subtract))
            dve.tensor_copy(keep["blocks"][:, 0, :], nb[:, :])
            dve.tensor_copy(keep["blocks"][:, 1, :], ends[:, :])
            chain(dve.tensor_scalar(ends[:, :], ends[:, :], float(P), None, ALU.mult))
            chain(dve.tensor_tensor(dest[:, :, :], dest[:, :, :], middle(ends[:, :], NT), ALU.add))
            for k in range(2):
                chain(dve.tensor_tensor(tmp[:, :, :], dest[:, :, :], keep["hot"][:, :, k, :], ALU.mult))
                chain(dve.tensor_reduce(slotf[:, :, k], tmp[:, :, :], AX, ALU.add))
            dve.tensor_copy(keep["slot"][:, :, :], slotf[:, :, :]).then_inc(s_slots, 1)


def experts(nc, io, dr, keep):
    with ExitStack() as ctx:
        m = Pool(nc, ctx, "ex")
        wg = [m.sb(f"wg{x}", [P, KC, DE]) for x in range(2)]
        wu = [m.sb(f"wu{x}", [P, KC, DE]) for x in range(2)]
        wd = [m.sb(f"wd{x}", [P, DE // P, D]) for x in range(2)]
        s_w = [m.sem(f"w{x}") for x in range(2)]

        def weights(sp, e, x):
            for dst, src in ((wg[x], io["w_exp_gate"]), (wu[x], io["w_exp_up"]), (wd[x], io["w_exp_down"])):
                sp.dma_start(dst[:, :, :], src[0, e].rearrange("a (k p) n -> p (a k) n", p=P)).then_inc(s_w[x], 16)

        dispatch(nc, io, dr, keep, lambda sp: [weights(sp, bass.ds(x, 1), x) for x in range(2)])

        ident = m.sb("ident", [P, P])
        cols = m.sb("cols", [P, PC_N])
        idx = m.sb("idx", [P, 1], U32)
        xb = m.sb("xb", [P, D])
        xT = m.sb("xT", [P, KC, P])
        sg = m.sb("sg", [P, DE])
        hh = m.sb("hh", [P, DE])
        hT = m.sb("hT", [P, DE // P, P])
        yb = m.sb("yb", [P, D])
        px = m.ps("px", [P, KC, P])
        pg = m.ps("pg", [P, DE])
        pu = m.ps("pu", [P, DE])
        phT = m.ps("phT", [P, 2, DE])
        py = m.ps("py", [P, 2, 512])
        s_const = m.sem("const")
        s_done = m.sem("done")
        s_idx = m.sem("idx_ld")
        s_x = m.sem("x")
        s_px = m.sem("px_done")
        s_xT = m.sem("xT_done")
        s_pg = m.sem("pg_done")
        s_pu = m.sem("pu_done")
        s_sg = m.sem("sg_done")
        s_hh = m.sem("hh_done")
        s_phT = m.sem("phT_done")
        s_hT = m.sem("hT_done")
        s_py = m.sem("py_done")
        s_yb = m.sem("yb_done")
        o_y = m.sem("o_y")
        s_apart = m.sem("apart")
        s_apart_pe = m.sem("apart_pe")
        block = ctx.enter_context(nc.Block())

        CHUNKS = (range(0, 1), range(1, DE // P))
        PARTS = (slice(0, P), slice(P, DE))

        def turns(eng, body, before=None, past=None):
            with eng.Fori(0, NE // 2) as i:
                for x in range(2):
                    n = eng.value_load(keep["blocks"][0:1, 0, bass.ds(2 * i + x, 1)], min_val=1, max_val=NT)
                    first = eng.value_load(keep["blocks"][0:1, 1, bass.ds(2 * i + x, 1)], min_val=0, max_val=NB - 2)
                    if before:
                        before(i, x)
                    with eng.Fori(0, n) as j:
                        body(nc.s_assert_within(first + j, 0, NB - 2, skip_runtime_bounds_check_because="the experts' blocks add up to less than NB"), x)
                    if past:
                        past()

        @block.sync
        def _(sp):
            sp.dma_start(ident[:, :], io["c_ident"]).then_inc(s_const, 16)
            sp.dma_start(cols[:, :], io["cols"]).then_inc(s_const, 16)
            with sp.Fori(0, NE // 2 - 1) as i:
                for x in range(2):
                    sp.wait_ge(s_done, 2 * i + x + 1)
                    weights(sp, bass.ds(2 * i + x + 2, 1), x)

        @block.gpsimd
        def _(pool):
            def gather(b):
                pool.dma_start(idx[:, :], dr["slot_tok"][bass.ds(b * P, P), :]).then_inc(s_idx, 16)
                pool.wait_ge(s_idx, 16 * b + 16)
                pool.sem_inc(s_apart, 1)
                pool.indirect_dma_start(xb[:, :], None, dr["hn"], bass.IndirectOffsetOnAxis(idx[:, 0:1], 0))\
                    .then_inc(s_x, 16)

            def body(b, x):
                pool.wait_ge(s_px, b + 1)
                pool.sem_inc(s_apart, 1)
                gather(b + 1)

            gather(0)
            turns(pool, body)

        @block.tensor
        def _(pe):
            def transpose_x(ks):
                for k in ks:
                    ins = pe.transpose(px[:, k, :], xb[:, k * P:(k + 1) * P], ident[:, :])
                return ins

            def transpose_h(ks, part):
                for k in ks:
                    ins = pe.transpose(phT[:, part, k * P:(k + 1) * P], hh[:, k * P:(k + 1) * P], ident[:, :])
                ins.then_inc(s_phT, 1)

            def body(b, x):
                pe.wait_ge(s_xT, b + 1)
                pe.wait_ge(s_hh, 2 * b + 2)
                for out, w, done in ((pg, wg[x], s_pg), (pu, wu[x], s_pu)):
                    for k in range(KC):
                        ins = pe.matmul(out[:, :], xT[:, k, :], w[:, k, :], start=(k == 0), stop=(k == KC - 1))
                    ins.then_inc(done, 1)
                pe.wait_ge(s_x, 16 * b + 32)
                transpose_x(range(KC - 2))
                pe.wait_ge(s_hh, 2 * b + 3)
                pe.wait_ge(s_hT, 2 * b + 2)
                transpose_h(CHUNKS[0], 0)
                transpose_x(range(KC - 2, KC)).then_inc(s_px, 1)
                pe.wait_ge(s_hh, 2 * b + 4)
                transpose_h(CHUNKS[1], 1)
                pe.wait_ge(s_yb, b + 1)
                for part in range(2):
                    pe.wait_ge(s_hT, 2 * b + 3 + part)
                    for n in range(2):
                        for k in CHUNKS[part]:
                            ins = pe.matmul(py[:, n, :], hT[:, k, :], wd[x][:, k, 512 * n:512 * n + 512],
                                            start=(k == 0), stop=(k == DE // P - 1))
                ins.then_inc(s_py, 1)

            def before(i, x):
                pe.wait_ge(s_w[x], 48 * i + 48)
                pe.sem_inc(s_apart_pe, 1)

            pe.wait_ge(s_const, 32)
            pe.wait_ge(s_x, 16)
            transpose_x(range(KC)).then_inc(s_px, 1)
            turns(pe, body, before)

        @block.scalar
        def _(act):
            def body(b, x):
                act.wait_ge(s_pg, b + 1)
                act.activation(sg[:, :], pg[:, :], ACT.Silu).then_inc(s_sg, 1)
                for part, at in enumerate(PARTS):
                    act.wait_ge(s_phT, 2 * b + 1 + part)
                    act.activation(hT[:, :, :].rearrange("p a n -> p (a n)")[:, at], phT[:, part, at], ACT.Copy)\
                        .then_inc(s_hT, 1)
                act.wait_ge(s_py, b + 1)
                act.wait_ge(o_y, 16 * b + 16)
                act.activation(yb[:, :], py[:, :, :].rearrange("p a n -> p (a n)"), ACT.Copy).then_inc(s_yb, 1)
                act.wait_ge(s_yb, b + 2)
                act.dma_start(dr["slots"][bass.ds(b * P, P), :], yb[:, :]).then_inc(o_y, 16)

            act.sem_inc(s_hT, 2)
            act.sem_inc(s_yb, 1)
            act.sem_inc(o_y, 16)
            turns(act, body, past=lambda: act.sem_inc(s_done, 1))
            last = act.value_load(keep["blocks"][0:1, 1, NE - 1:NE], min_val=0, max_val=NB - 2)
            n = act.value_load(keep["blocks"][0:1, 0, NE - 1:NE], min_val=1, max_val=NT)
            act.wait_ge(o_y, 16 * last + 16 * n + 16)
            act.sem_inc(s_const, 1)

        @block.vector
        def _(dve):
            def copy_x(b):
                dve.tensor_tensor(xT[:, :, :], px[:, :, :], wide(cols[:, PC_LN2:PC_LN2 + KC], P), ALU.mult).then_inc(s_xT, 1)

            def body(b, x):
                dve.wait_ge(s_sg, b + 1)
                dve.wait_ge(s_pu, b + 1)
                for at in PARTS:
                    dve.tensor_tensor(hh[:, at], sg[:, at], pu[:, at], ALU.mult).then_inc(s_hh, 1)
                dve.wait_ge(s_px, b + 2)
                copy_x(b + 1)

            dve.sem_inc(s_hh, 2)
            dve.wait_ge(s_const, 32)
            dve.wait_ge(s_px, 1)
            copy_x(0)
            turns(dve, body)

    with ExitStack() as ctx:
        m = Pool(nc, ctx, "cb")
        ya = [m.sb(f"ya{x}", [P, 2, D]) for x in range(2)]
        hb = [m.sb(f"hb{x}", [P, D]) for x in range(2)]
        acc = [m.sb(f"acc{x}", [P, D]) for x in range(2)]
        s_y = [m.sem(f"y{x}") for x in range(2)]
        s_h = [m.sem(f"h{x}") for x in range(2)]
        s_acc = m.sem("acc_done")
        s_ch = m.sem("chain")
        o_out = [m.sem(f"o_out{x}") for x in range(2)]
        block = ctx.enter_context(nc.Block())

        @block.gpsimd
        def _(pool):
            for t in range(NT):
                if t >= 2:
                    pool.wait_ge(s_acc, t - 1)
                for n in range(2):
                    pool.indirect_dma_start(ya[t % 2][:, n, :], None, dr["slots"],
                                            bass.IndirectOffsetOnAxis(keep["slot"][:, t, n:n + 1], 0)).then_inc(s_y[t % 2], 16)

        @block.sync
        def _(sp):
            for t in range(NT):
                if t >= 2:
                    sp.wait_ge(s_acc, t - 1)
                sp.dma_start(hb[t % 2][:, :], dr["h"][t * P:(t + 1) * P, :]).then_inc(s_h[t % 2], 16)

        @block.scalar
        def _(act):
            for t in range(NT):
                act.wait_ge(s_acc, t + 1)
                act.dma_start(io["out"][0, t * P:(t + 1) * P, :], acc[t % 2][:, :]).then_inc(o_out[t % 2], 16)
            for x in range(2):
                act.wait_ge(o_out[x], 16 * NT // 2)

        @block.vector
        def _(dve):
            for t in range(NT):
                x = t % 2
                dve.wait_ge(s_y[x], 32 * (t // 2) + 32)
                dve.wait_ge(s_h[x], 16 * (t // 2) + 16)
                dve.scalar_tensor_tensor(hb[x][:, :], ya[x][:, 0, :], keep["gate"][:, t, 0:1], hb[x][:, :],
                                         ALU.mult, ALU.add).then_inc(s_ch, 1)
                dve.wait_ge(s_ch, t + 1)
                if t >= 2:
                    dve.wait_ge(o_out[x], 16 * (t // 2))
                dve.scalar_tensor_tensor(acc[x][:, :], ya[x][:, 1, :], keep["gate"][:, t, 1:2], hb[x][:, :],
                                         ALU.mult, ALU.add).then_inc(s_acc, 1)


def build(nc, io, out):
    def scratch(name, shape, dt=F32):
        return nc.dram_tensor(name, shape, dt).ap()

    dr = {
        "qk": scratch("qk_s", [8, P, S]), "v": scratch("v_s", [S, DA]),
        "chunks": scratch("chunks_s", [NCH, P, NPAIR, ROW]),
        "o": scratch("o_s", [S, DA]), "y": scratch("y_s", [NPAIR, P, S]),
        "h": scratch("h_s", [S, D]), "hn": scratch("hn_s", [S, D]),
        "slot_tok": scratch("slot_tok_s", [NB * P, 1], I32), "slots": scratch("slots_s", [NB * P, D]),
        "bonus": scratch("bonus_s", [NPAIR, P, S]), "g": scratch("g_s", [NPAIR, P, S]),
    }
    io["out"] = out
    with ExitStack() as ctx:
        m = Pool(nc, ctx, "keep")
        keep = {
            "hot": m.sb("hot", [P, NT, 2, NE]),
            "gate": m.sb("gate", [P, NT, 2]),
            "slot": m.sb("slot", [P, NT, 2], U32),
            "blocks": m.sb("blocks", [P, 2, NE], I32),
        }
        project(nc, io, dr)
        attend(nc, io, dr)
        recur(nc, io, dr)
        merge(nc, io, dr, keep)
        experts(nc, io, dr, keep)


def constants():
    half = 8
    inv = np.float32(500000.0) ** (-np.arange(0, 16, 2, dtype=np.float32) / np.float32(16))
    ang = (np.arange(S, dtype=np.float32)[:, None] * inv[None, :].astype(np.float32)).astype(np.float32)
    cos, sin = np.cos(ang).T, np.sin(ang).T
    cosin = np.zeros((P, 2, S), np.float32)
    cosin[:, 0] = 1.0
    swap = np.zeros((P, P), np.float32)
    for b in (0, 64):
        cosin[b:b + half, 0] = cosin[b + half:b + 2 * half, 0] = cos
        cosin[b:b + half, 1] = -sin
        cosin[b + half:b + 2 * half, 1] = sin
        for i in range(half):
            swap[b + i, b + half + i] = swap[b + half + i, b + i] = 1.0
    ones2 = np.kron(np.eye(2), np.ones((64, 64))).astype(np.float32)
    mask = np.zeros((P, 2, P), np.float32)
    mask[0, 0, 0:C] = -1e30
    mask[0, 1, C:] = 1.0
    row, col = np.arange(P)[:, None] % C, np.arange(C)[None, :]
    one = lambda a: a.astype(np.float32)
    past = one(row <= col)
    mgb = np.concatenate([one((row < col) & (row // 16 == col // 16)), past], 1)
    mgk = np.concatenate([one(row < col), past], 1)
    mgl = np.stack([one((col < row) & (row // 16 == col // 16)),
                    one((row // 32 == col // 32) & (row // 16 > col // 16)), one(row // 32 > col // 32)], 1)
    reset = np.ones((P, GT), np.float32)
    reset[:, ::C] = 0.0
    return {"c_ident": np.eye(P, dtype=np.float32), "c_ones2": ones2, "c_swap": swap, "c_cosin": cosin,
            "c_reset": reset, "c_mean2": ones2 / 64,
            "c_giota": np.ascontiguousarray(np.broadcast_to(np.arange(NE, dtype=np.float32) // EPG, (P, NE))),
            "c_eiota": np.ascontiguousarray(np.broadcast_to(np.arange(NE, dtype=np.float32), (P, NE))),
            "c_before": np.triu(np.ones((P, P), np.float32), 1), "c_ones": np.ones((P, P), np.float32),
            "c_blocks": np.ascontiguousarray(np.broadcast_to(P * np.arange(1, NT + 1, dtype=np.float32), (P, NT))),
             "c_mask": mask,
            "c_eye": one(row == col), "c_mgb": mgb, "c_mgk": mgk, "c_mgl": mgl}


def kernel(**inputs):
    import concourse.bacc as _bacc
    from concourse.bass_utils import run_bass_kernel_spmd as _run

    def col(name):
        a = np.asarray(inputs[name])[0]
        return a.reshape(-1, P).T

    arrays = {n: np.ascontiguousarray(inputs[n]) for n in
              ("w_in", "w_lora_up", "a_lora_up", "g_lora_up", "w_out", "w_exp_gate", "w_exp_up", "w_exp_down")}
    x = np.asarray(inputs["x"])[0]
    arrays["x"] = np.concatenate([x, np.zeros((2 * GT, D), x.dtype)])
    twice = lambda n: np.concatenate([np.asarray(inputs[n])[0]] * 2).reshape(P, 1)
    arrays["cols"] = np.ascontiguousarray(np.concatenate(
        [col(n) for n in ("ln1_g", "shift_mu", "w0", "a0", "k_k", "k_a", "r_k", "ln_x_g", "ln_x_b", "ln2_g")]
        + [twice("q_norm_g"), twice("k_norm_g")], axis=1))
    both = np.concatenate([np.asarray(inputs["w_router_group"])[0], np.asarray(inputs["w_router_expert"])[0]], 1)
    arrays["w_rt"] = np.ascontiguousarray(both.reshape(KC, P, 4 + NE).transpose(1, 0, 2))
    both = np.concatenate([np.asarray(inputs["b_router_group"])[0], np.asarray(inputs["b_router_expert"])[0]])
    arrays["b_rt"] = np.ascontiguousarray(np.broadcast_to(both, (P, 4 + NE)))
    arrays["subln"] = np.ascontiguousarray(np.broadcast_to(np.asarray(inputs["subln_g"])[0], (P, P)))
    lams = np.stack([np.asarray(inputs[n])[0] for n in ("lambda_q1", "lambda_k1", "lambda_q2", "lambda_k2")])
    arrays["lams"] = np.ascontiguousarray(np.broadcast_to(lams, (P, 4, 64)))
    arrays.update(constants())
    nc = _bacc.Bacc("TRN2", target_bir_lowering=False, num_devices=1)
    io = {n: nc.dram_tensor(f"in_{n}", a.shape, mybir.dt.from_np(a.dtype), kind="ExternalInput").ap()
          for n, a in arrays.items()}
    out = nc.dram_tensor("out_0", (1, S, D), F32, kind="ExternalOutput").ap()
    build(nc, io, out)
    r = _run(nc, [{f"in_{n}": a for n, a in arrays.items()}], core_ids=[0])
    return r.results[0]["out_0"]
```
